# Optimizing a Trainium2 kernel written in Bass

```python
import math
import jax, jax.numpy as jnp
from jax import lax
import numpy as np

D_MODEL = 1024
BATCH = 1
SEQ = 256
DEPTH = 2

GRID_W = 64
CTX_LEN = 256
EPS = 1e-6
CONV_WIDTH = 3

GDN_HEADS = 8
GDN_DK = 128
GDN_DV = 128
GDN_CHUNK = 64
GDN_QK_DIM = GDN_HEADS * GDN_DK
GDN_V_DIM = GDN_HEADS * GDN_DV
GDN_QKV = 2 * GDN_QK_DIM + GDN_V_DIM

SSD_D_INNER = D_MODEL
SSD_HEAD_DIM = 64
SSD_HEADS = SSD_D_INNER // SSD_HEAD_DIM
SSD_GROUPS = 2
SSD_HEADS_PER_GROUP = SSD_HEADS // SSD_GROUPS
SSD_STATE = 128
SSD_CHUNK = 128
SSD_XBC = SSD_D_INNER + 2 * SSD_GROUPS * SSD_STATE

ATT_HEADS = 8
ATT_KV_HEADS = 2
ATT_REP = ATT_HEADS // ATT_KV_HEADS
ATT_HEAD_DIM = 128
ATT_BLOCK = 128
ATT_Q_DIM = ATT_HEADS * ATT_HEAD_DIM
ATT_KV_DIM = ATT_KV_HEADS * ATT_HEAD_DIM
ROPE_THETA = 10000.0

N_BRANCHES = 3
D_FF = 4 * D_MODEL

SPLIT_SIZES = (GDN_QKV, GDN_V_DIM, 2 * GDN_HEADS, 2 * GDN_HEADS,
               SSD_D_INNER, SSD_XBC, 2 * SSD_HEADS,
               ATT_Q_DIM, 2 * ATT_KV_DIM,
               N_BRANCHES * D_MODEL)
D_IN = sum(SPLIT_SIZES)

kernel_name = 'hybrid_gdn_ssd_gqa_prefix_dit'

def rms_norm(x, w):
    xf = x.astype(jnp.float32)
    y = xf * lax.rsqrt(jnp.mean(xf * xf, axis=-1, keepdims=True) + EPS)
    return (y * w.astype(jnp.float32)).astype(x.dtype)

def l2_norm(x):
    xf = x.astype(jnp.float32)
    return xf * lax.rsqrt(jnp.sum(xf * xf, axis=-1, keepdims=True) + EPS)

def flip(t):
    return jnp.flip(t, axis=1)

def split_in_proj(p):
    out, start = [], 0
    for size in SPLIT_SIZES:
        out.append(p[..., start:start + size])
        start += size
    return out

def depthwise_conv(x, w, b=None):
    k_w, ch = w.shape
    y = lax.conv_general_dilated(x, w[:, None, :].astype(x.dtype), window_strides=(1,),
                                 padding=[(k_w // 2, k_w // 2)],
                                 dimension_numbers=('NWC', 'WIO', 'NWC'),
                                 feature_group_count=ch)
    if b is not None:
        y = y + b.astype(x.dtype)
    return y

def rope_axis(t, pos):
    h = t.shape[-1] // 2
    freqs = ROPE_THETA ** (-jnp.arange(h, dtype=jnp.float32) / h)
    ang = pos.astype(jnp.float32)[:, None] * freqs[None, :]
    cos = jnp.cos(ang)[None, :, None, :]
    sin = jnp.sin(ang)[None, :, None, :]
    tf = t.astype(jnp.float32)
    t1, t2 = tf[..., :h], tf[..., h:]
    return jnp.concatenate([t1 * cos - t2 * sin, t1 * sin + t2 * cos], axis=-1)

def rope_2d(x, rows, cols):
    half = x.shape[-1] // 2
    return jnp.concatenate([rope_axis(x[..., :half], rows),
                            rope_axis(x[..., half:], cols)], axis=-1).astype(x.dtype)

def gdn_chunked(q, k, v, log_a, beta, s0):
    bsz, seq_len, n_h, dk = q.shape
    dv = v.shape[-1]
    n_c = seq_len // GDN_CHUNK

    def chunks(t):
        t = t.reshape((bsz, n_c, GDN_CHUNK, n_h) + t.shape[3:])
        return jnp.swapaxes(t, 2, 3)

    q = chunks(q * dk ** -0.5)
    k = chunks(k)
    v = chunks(v)
    beta = chunks(beta)
    g = jnp.cumsum(chunks(log_a), axis=-1)
    idx = jnp.arange(GDN_CHUNK)
    incl = idx[:, None] >= idx[None, :]
    strict = idx[:, None] > idx[None, :]
    decay = jnp.exp(jnp.where(incl, g[..., :, None] - g[..., None, :], -jnp.inf))
    k_beta = k * beta[..., None]
    a_mat = jnp.where(strict, jnp.einsum('bnhid,bnhjd->bnhij', k_beta, k) * decay, 0.0)
    eye = jnp.eye(GDN_CHUNK, dtype=jnp.float32)
    rhs = jnp.concatenate([v * beta[..., None], k_beta * jnp.exp(g)[..., None]], axis=-1)
    sol = lax.linalg.triangular_solve(a_mat + eye, rhs, left_side=True, lower=True)
    u, w = sol[..., :dv], sol[..., dv:]
    qk = jnp.where(incl, jnp.einsum('bnhid,bnhjd->bnhij', q, k) * decay, 0.0)
    q_dec = q * jnp.exp(g)[..., None]
    k_dec = k * jnp.exp(g[..., -1:] - g)[..., None]
    chunk_decay = jnp.exp(g[..., -1])

    def step(state, xs):
        qk_c, u_c, w_c, qd_c, kd_c, cd_c = xs
        v_new = u_c - jnp.einsum('bhcd,bhde->bhce', w_c, state)
        o_c = jnp.einsum('bhcd,bhde->bhce', qd_c, state) + jnp.einsum('bhij,bhje->bhie', qk_c, v_new)
        state = state * cd_c[..., None, None] + jnp.einsum('bhcd,bhce->bhde', kd_c, v_new)
        return state, o_c

    xs = tuple(jnp.moveaxis(t, 1, 0) for t in (qk, u, w, q_dec, k_dec, chunk_decay))
    s_final, o = lax.scan(step, s0, xs)
    o = jnp.transpose(o, (1, 0, 3, 2, 4)).reshape(bsz, seq_len, n_h, dv)
    return o, s_final

def gdn_branch(qkv, z, beta_raw, a_raw, conv_w, a_log, dt_bias, norm_w, s0_f, s0_b):
    bsz, seq_len, _ = qkv.shape
    qkv = jax.nn.silu(depthwise_conv(qkv, conv_w))
    q = l2_norm(qkv[..., :GDN_QK_DIM].reshape(bsz, seq_len, GDN_HEADS, GDN_DK))
    k = l2_norm(qkv[..., GDN_QK_DIM:2 * GDN_QK_DIM].reshape(bsz, seq_len, GDN_HEADS, GDN_DK))
    v = qkv[..., 2 * GDN_QK_DIM:].reshape(bsz, seq_len, GDN_HEADS, GDN_DV).astype(jnp.float32)
    beta = jax.nn.sigmoid(beta_raw.astype(jnp.float32)).reshape(bsz, seq_len, 2, GDN_HEADS)
    log_a = -jnp.exp(a_log.astype(jnp.float32)) * jax.nn.softplus(
        a_raw.astype(jnp.float32).reshape(bsz, seq_len, 2, GDN_HEADS) + dt_bias.astype(jnp.float32))
    o_f, s_f = gdn_chunked(q, k, v, log_a[:, :, 0], beta[:, :, 0], s0_f)
    o_b, s_b = gdn_chunked(flip(q), flip(k), flip(v), flip(log_a[:, :, 1]), flip(beta[:, :, 1]), s0_b)
    o = o_f + flip(o_b)
    o = rms_norm(o, norm_w) * jax.nn.silu(z.astype(jnp.float32).reshape(bsz, seq_len, GDN_HEADS, GDN_DV))
    return o.reshape(bsz, seq_len, GDN_V_DIM).astype(qkv.dtype), s_f, s_b

def ssd_chunked(x, dt, a, bm, cm, s0):
    bsz, seq_len = x.shape[:2]
    n_c = seq_len // SSD_CHUNK

    def chunks(t):
        return t.reshape((bsz, n_c, SSD_CHUNK) + t.shape[2:])

    xdt = chunks(x * dt[..., None])
    bm = chunks(bm)
    cm = chunks(cm)
    a_cs = jnp.moveaxis(jnp.cumsum(chunks(dt * a), axis=2), 2, -1)
    idx = jnp.arange(SSD_CHUNK)
    incl = idx[:, None] >= idx[None, :]
    l_mat = jnp.exp(jnp.where(incl, a_cs[..., :, None] - a_cs[..., None, :], -jnp.inf))
    cb = jnp.einsum('bcign,bcjgn->bcgij', cm, bm)
    y_diag = jnp.einsum('bcgij,bcgeij,bcjgep->bcigep', cb, l_mat, xdt)
    decay_to_end = jnp.exp(a_cs[..., -1:] - a_cs)
    states = jnp.einsum('bcjgn,bcgej,bcjgep->bcgepn', bm, decay_to_end, xdt)
    chunk_decay = jnp.exp(a_cs[..., -1])

    def step(state, xs):
        st, cd = xs
        return state * cd[..., None, None] + st, state

    s_final, s_prev = lax.scan(step, s0, (jnp.moveaxis(states, 1, 0), jnp.moveaxis(chunk_decay, 1, 0)))
    s_prev = jnp.moveaxis(s_prev, 0, 1)
    y_off = jnp.einsum('bcign,bcgepn,bcgei->bcigep', cm, s_prev, jnp.exp(a_cs))
    return (y_diag + y_off).reshape(x.shape), s_final

def ssd_branch(z, xbc, dt_raw, conv_w, conv_b, a_log, dt_bias, d_skip, norm_w, s0_f, s0_b):
    bsz, seq_len, _ = xbc.shape
    gn = SSD_GROUPS * SSD_STATE
    xbc = jax.nn.silu(depthwise_conv(xbc, conv_w, conv_b)).astype(jnp.float32)
    xs = xbc[..., :SSD_D_INNER].reshape(bsz, seq_len, SSD_GROUPS, SSD_HEADS_PER_GROUP, SSD_HEAD_DIM)
    bm = xbc[..., SSD_D_INNER:SSD_D_INNER + gn].reshape(bsz, seq_len, SSD_GROUPS, SSD_STATE)
    cm = xbc[..., SSD_D_INNER + gn:].reshape(bsz, seq_len, SSD_GROUPS, SSD_STATE)
    dt = jax.nn.softplus(
        dt_raw.astype(jnp.float32).reshape(bsz, seq_len, 2, SSD_GROUPS, SSD_HEADS_PER_GROUP)
        + dt_bias.astype(jnp.float32).reshape(2, SSD_GROUPS, SSD_HEADS_PER_GROUP))
    a = -jnp.exp(a_log.astype(jnp.float32)).reshape(2, SSD_GROUPS, SSD_HEADS_PER_GROUP)
    y_f, s_f = ssd_chunked(xs, dt[:, :, 0], a[0], bm, cm, s0_f)
    y_b, s_b = ssd_chunked(flip(xs), flip(dt[:, :, 1]), a[1], flip(bm), flip(cm), s0_b)
    y = y_f + flip(y_b) + d_skip.astype(jnp.float32).reshape(SSD_GROUPS, SSD_HEADS_PER_GROUP, 1) * xs
    y = y.reshape(bsz, seq_len, SSD_D_INNER) * jax.nn.silu(z.astype(jnp.float32))
    y = rms_norm(y.reshape(bsz, seq_len, SSD_GROUPS, SSD_D_INNER // SSD_GROUPS),
                 norm_w.reshape(SSD_GROUPS, SSD_D_INNER // SSD_GROUPS))
    return y.reshape(bsz, seq_len, SSD_D_INNER).astype(z.dtype), s_f, s_b

def att_q(q_raw, q_norm):
    bsz, seq_len, _ = q_raw.shape
    return rms_norm(q_raw.reshape(bsz, seq_len, ATT_HEADS, ATT_HEAD_DIM), q_norm)

def att_kv(kv_raw, k_norm):
    bsz, seq_len, _ = kv_raw.shape
    kv = kv_raw.reshape(bsz, seq_len, 2, ATT_KV_HEADS, ATT_HEAD_DIM)
    return rms_norm(kv[:, :, 0], k_norm), kv[:, :, 1]

def gqa_blocks(q, k, v):
    bsz, lq = q.shape[:2]
    n_b = lq // ATT_BLOCK
    q = q.reshape(bsz, n_b, ATT_BLOCK, ATT_KV_HEADS, ATT_REP, ATT_HEAD_DIM)
    qb = jnp.moveaxis(q, 1, 0)
    scale = ATT_HEAD_DIM ** -0.5

    def one_block(q_blk):
        s = jnp.einsum('bqgrd,bkgd->bgrqk', q_blk, k).astype(jnp.float32) * scale
        p = jax.nn.softmax(s, axis=-1).astype(v.dtype)
        return jnp.einsum('bgrqk,bkgd->bqgrd', p, v)

    o = lax.map(one_block, qb)
    return jnp.moveaxis(o, 0, 1).reshape(bsz, lq, ATT_Q_DIM)

def merge_branches(y_gdn, y_ssd, y_att, gates, w_br_gdn, w_br_ssd, w_br_att, w_out):
    g = jax.nn.sigmoid(gates.astype(jnp.float32)).astype(y_gdn.dtype)
    g_gdn, g_ssd, g_att = jnp.split(g, N_BRANCHES, axis=-1)
    m = g_gdn * (y_gdn @ w_br_gdn) + g_ssd * (y_ssd @ w_br_ssd) + g_att * (y_att @ w_br_att)
    return m @ w_out

def mixing_sublayer(h, hc, rows, cols, with_ctx_out, w_in, gdn_conv, gdn_a_log, gdn_dt_bias, gdn_norm,
                    ssd_conv_w, ssd_conv_b, ssd_a_log, ssd_dt_bias, ssd_d, ssd_norm,
                    att_q_norm, att_k_norm, w_br_gdn, w_br_ssd, w_br_att, w_out):
    bsz, seq_len, _ = h.shape
    p_lat = split_in_proj(h @ w_in)
    p_ctx = split_in_proj(hc @ w_in)
    gdn_p = (gdn_conv, gdn_a_log, gdn_dt_bias, gdn_norm)
    ssd_p = (ssd_conv_w, ssd_conv_b, ssd_a_log, ssd_dt_bias, ssd_d, ssd_norm)
    zeros_gdn = jnp.zeros((bsz, GDN_HEADS, GDN_DK, GDN_DV), jnp.float32)
    zeros_ssd = jnp.zeros((bsz, SSD_GROUPS, SSD_HEADS_PER_GROUP, SSD_HEAD_DIM, SSD_STATE), jnp.float32)

    gdn_c, sg_f, sg_b = gdn_branch(*p_ctx[0:4], *gdn_p, zeros_gdn, zeros_gdn)
    ssd_c, ss_f, ss_b = ssd_branch(*p_ctx[4:7], *ssd_p, zeros_ssd, zeros_ssd)
    k_c, v_c = att_kv(p_ctx[8], att_k_norm)

    gdn_l, _, _ = gdn_branch(*p_lat[0:4], *gdn_p, sg_f, sg_b)
    ssd_l, _, _ = ssd_branch(*p_lat[4:7], *ssd_p, ss_f, ss_b)
    q_l = rope_2d(att_q(p_lat[7], att_q_norm), rows, cols)
    k_l, v_l = att_kv(p_lat[8], att_k_norm)
    k_l = rope_2d(k_l, rows, cols)
    att_l = gqa_blocks(q_l, jnp.concatenate([k_c, k_l], axis=1), jnp.concatenate([v_c, v_l], axis=1))
    y_lat = merge_branches(gdn_l, ssd_l, att_l, p_lat[9], w_br_gdn, w_br_ssd, w_br_att, w_out)

    y_ctx = None
    if with_ctx_out:
        att_c = gqa_blocks(att_q(p_ctx[7], att_q_norm), k_c, v_c)
        y_ctx = merge_branches(gdn_c, ssd_c, att_c, p_ctx[9], w_br_gdn, w_br_ssd, w_br_att, w_out)
    return y_lat, y_ctx

def sq_relu_mlp(h, w1, w2):
    return jnp.square(jax.nn.relu(h @ w1)) @ w2

def setup_inputs(seed: int = 0) -> dict:
    key = jax.random.key(seed)
    k = jax.random.split(key, 27)
    f32 = jnp.float32

    def nrm(i, shape, scale):
        return scale * jax.random.normal(k[i], shape, f32)

    def gain(i, shape):
        return 1.0 + 0.02 * jax.random.normal(k[i], shape, f32)

    def a_log(i, n):
        return jnp.log(jax.random.uniform(k[i], (DEPTH, 2, n), f32, 1.0, 16.0))

    def dt_bias(i, n):
        dt = jnp.exp(jax.random.uniform(k[i], (DEPTH, 2, n), f32, math.log(1e-3), math.log(1e-1)))
        return dt + jnp.log(-jnp.expm1(-dt))

    return {
        'x': nrm(0, (BATCH, SEQ, D_MODEL), 1.0),
        'c': nrm(1, (BATCH, D_MODEL), 1.0),
        'ctx': nrm(2, (BATCH, CTX_LEN, D_MODEL), 1.0),
        'c_ctx': nrm(3, (D_MODEL,), 1.0),
        'w_mod': nrm(4, (DEPTH, D_MODEL, 6 * D_MODEL), 0.5 * D_MODEL ** -0.5),
        'b_mod': nrm(5, (DEPTH, 6 * D_MODEL), 0.02),
        'norm_mix': gain(6, (DEPTH, D_MODEL)),
        'norm_mlp': gain(7, (DEPTH, D_MODEL)),
        'w_in': nrm(8, (DEPTH, D_MODEL, D_IN), D_MODEL ** -0.5),
        'gdn_conv': nrm(9, (DEPTH, CONV_WIDTH, GDN_QKV), CONV_WIDTH ** -0.5),
        'gdn_a_log': a_log(10, GDN_HEADS),
        'gdn_dt_bias': dt_bias(11, GDN_HEADS),
        'gdn_norm': gain(12, (DEPTH, GDN_DV)),
        'ssd_conv_w': nrm(13, (DEPTH, CONV_WIDTH, SSD_XBC), CONV_WIDTH ** -0.5),
        'ssd_conv_b': nrm(14, (DEPTH, SSD_XBC), 0.02),
        'ssd_a_log': a_log(15, SSD_HEADS),
        'ssd_dt_bias': dt_bias(16, SSD_HEADS),
        'ssd_d': gain(17, (DEPTH, SSD_HEADS)),
        'ssd_norm': gain(18, (DEPTH, SSD_D_INNER)),
        'att_q_norm': gain(19, (DEPTH, ATT_HEAD_DIM)),
        'att_k_norm': gain(20, (DEPTH, ATT_HEAD_DIM)),
        'w_br_gdn': nrm(21, (DEPTH, GDN_V_DIM, D_MODEL), GDN_V_DIM ** -0.5),
        'w_br_ssd': nrm(22, (DEPTH, SSD_D_INNER, D_MODEL), SSD_D_INNER ** -0.5),
        'w_br_att': nrm(23, (DEPTH, ATT_Q_DIM, D_MODEL), ATT_Q_DIM ** -0.5),
        'w_out': nrm(24, (DEPTH, D_MODEL, D_MODEL), D_MODEL ** -0.5),
        'w_ff1': nrm(25, (DEPTH, D_MODEL, D_FF), D_MODEL ** -0.5),
        'w_ff2': nrm(26, (DEPTH, D_FF, D_MODEL), D_FF ** -0.5),
    }

def reference(x, c, ctx, c_ctx, w_mod, b_mod, norm_mix, norm_mlp, w_in, gdn_conv, gdn_a_log, gdn_dt_bias,
              gdn_norm, ssd_conv_w, ssd_conv_b, ssd_a_log, ssd_dt_bias, ssd_d, ssd_norm, att_q_norm, att_k_norm,
              w_br_gdn, w_br_ssd, w_br_att, w_out, w_ff1, w_ff2):
    seq_len = x.shape[1]
    rows_n = seq_len // GRID_W
    rows = jnp.broadcast_to(jnp.arange(rows_n, dtype=jnp.int32)[:, None], (rows_n, GRID_W)).reshape(-1)
    cols = jnp.broadcast_to(jnp.arange(GRID_W, dtype=jnp.int32)[None, :], (rows_n, GRID_W)).reshape(-1)
    xc = ctx
    for l in range(DEPTH):
        last = l == DEPTH - 1
        sh1, sc1, g1, sh2, sc2, g2 = jnp.split((jax.nn.silu(c) @ w_mod[l] + b_mod[l])[:, None, :], 6, axis=-1)
        csh1, csc1, cg1, csh2, csc2, cg2 = jnp.split(jax.nn.silu(c_ctx) @ w_mod[l] + b_mod[l], 6, axis=-1)

        h = rms_norm(x, norm_mix[l]) * (1.0 + sc1) + sh1
        hc = rms_norm(xc, norm_mix[l]) * (1.0 + csc1) + csh1
        y, yc = mixing_sublayer(h, hc, rows, cols, not last, w_in[l], gdn_conv[l], gdn_a_log[l], gdn_dt_bias[l],
                                gdn_norm[l], ssd_conv_w[l], ssd_conv_b[l], ssd_a_log[l], ssd_dt_bias[l],
                                ssd_d[l], ssd_norm[l], att_q_norm[l], att_k_norm[l],
                                w_br_gdn[l], w_br_ssd[l], w_br_att[l], w_out[l])
        x = x + g1 * y
        h = rms_norm(x, norm_mlp[l]) * (1.0 + sc2) + sh2
        x = x + g2 * sq_relu_mlp(h, w_ff1[l], w_ff2[l])

        if not last:
            xc = xc + cg1 * yc
            hc = rms_norm(xc, norm_mlp[l]) * (1.0 + csc2) + csh2
            xc = xc + cg2 * sq_relu_mlp(hc, w_ff1[l], w_ff2[l])
    return x


_drawn_inputs = setup_inputs


def setup_inputs(seed=0):
    import zlib

    import numpy as np

    out = dict(_drawn_inputs(seed))
    spreads = {}
    factors = {'norm_mix': 6.876,
     'norm_mlp': 4.488,
     'gdn_norm': 8.0,
     'ssd_conv_b': 48.581,
     'ssd_d': 64.0,
     'ssd_norm': 61.312,
     'att_q_norm': 8.0,
     'att_k_norm': 8.0}
    for name, (base, spread) in spreads.items():
        noise = np.random.default_rng([zlib.crc32(name.encode()), seed]).standard_normal(out[name].shape)
        drawn = base * np.exp(spread * noise) if base else spread * noise
        out[name] = __import__('jax').numpy.asarray(drawn.astype(out[name].dtype))
    for name, factor in factors.items():
        out[name] = (out[name] * factor).astype(out[name].dtype)
    return out
```

```python
from contextlib import ExitStack, contextmanager

import concourse.bass as bass
import numpy as np
from concourse import mybir

F32 = mybir.dt.float32
BF16 = mybir.dt.bfloat16
ALU = mybir.AluOpType
ACT = mybir.ActivationFunctionType
AX_X = mybir.AxisListType.X

P = 128
DEPTH = 2
D_MODEL = 1024
KT = D_MODEL // P
SEG = 256
T = 2 * SEG
NT = T // P
EPS = 1e-6
RING = 8

GH = 8
SG = 2
SHG = 8
SH = SG * SHG
SHD = 64
AH = 8
AKV = 2
GRID_W = 64
LEVELS = 7

N_MOD, N_GDN, N_SSD, N_ATT, N_MERGE, N_OUT, N_FF1, N_FF2 = 48, 32, 20, 12, 48, 8, 32, 32
U_GDN, U_CONV, U_Z, U_ATT, U_MERGE, U_OUT, U_FF1, U_FF2 = 16, 6, 4, 6, 24, 4, 16, 4
USES = U_GDN + U_CONV + U_Z + U_ATT + U_MERGE + U_OUT + U_FF1 + U_FF2
PIECES = N_MOD + N_GDN + N_SSD + N_ATT + N_MERGE + N_OUT + N_FF1 + N_FF2

C_BMOD, C_NMIX, C_NMLP, C_GCONV, C_SCONV, C_SCONVB, C_SNORM, C_GNORM, C_QN, C_KN = (
    0, 48, 56, 64, 136, 172, 184, 192, 193, 194)
NPAR = 195
R_BIAS, R_ALOG, R_SKIP, NROW = 0, 48, 96, 112

K_ID, K_ONES, K_UF, K_UB, K_ROT, K_COS, K_SIN, K_EPS = 0, 128, 256, 384, 512, 640, 896, 1152
NCST = 1156
B_ID, B_NEG, B_M1T = 0, P, 3 * P
B_MASK = B_M1T + 2 * P
NCSTB = B_MASK + 2 * LEVELS * P

NEGG, NEGEG, EG, BETA, BDEC, CHUNK, LOGA = range(7)
NKIND = 7
VISIT = ((0, 1, 2, 3), (1, 0, 3, 2))


class Seen:

    def __init__(self, eng):
        self.eng, self.base, self.local, self.per, self.step = eng, {}, {}, None, None

    def skip(self, sem, k=1):
        self.local[sem.name] = self.local.get(sem.name, 0) + k

    def next(self, sem, k=1):
        self.skip(sem, k)
        value = self.base.get(sem.name, 0) + self.local[sem.name]
        if self.per is not None:
            value = self.step * self.per.get(sem.name, 0) + value
        return value

    @contextmanager
    def loop(self, count, per):
        self.base = {n: self.base.get(n, 0) + self.local.get(n, 0) for n in {*self.base, *self.local}}
        self.local, self.per = {}, per
        with self.eng.Fori(0, count) as i:
            self.step = i
            yield i
        left = {n: v for n, v in self.local.items() if v}
        assert left == {n: v for n, v in per.items() if v}, left
        for n, v in left.items():
            self.base[n] = self.base.get(n, 0) + count * v
        self.local, self.per, self.step = {}, None, None

    def upto(self, sem, total):
        self.local[sem.name] = total - self.base.get(sem.name, 0)
        return total


def build(nc, pieces, small_w, x_in, cvec, par_in, row_in, cst_in, masks_in, out):
    with ExitStack() as ctx:
        def sb(name, shape, dt=F32):
            return ctx.enter_context(nc.sbuf_tensor(name, shape, dt))

        def sem(name):
            return ctx.enter_context(nc.semaphore(name))

        X = sb("X", [P, KT, T])
        hT = sb("hT", [P, KT, T])
        ring = sb("ring", [P, RING, KT, P])
        arena = sb("arena", [P, 32 * T])
        work = sb("work", [P, 13312])
        cst = sb("cst", [P, NCST])
        cstb = sb("cstb", [P, NCSTB], BF16)
        par = sb("par", [P, DEPTH, NPAR])
        rowp = sb("rowp", [P, DEPTH, NROW])
        wsm = sb("wsm", [P, KT, 64])
        csil = sb("csil", [P, KT, 2])
        modv = sb("modv", [P, 48, 2])
        coefA = sb("coefA", [P, 2, KT, 2])
        rs = sb("rs", [P, T])
        PS = ctx.enter_context(nc.psum_tensor("PS", [P, 8, T], F32))

        aT = arena[:, :].rearrange("p (m t) -> p m t", m=32)
        yG, yS, yA, mT = (aT[:, 8 * j:8 * j + 8, :] for j in range(4))
        ident = cst[:, K_ID:K_ID + P]
        ones = cst[:, K_ONES:K_ONES + P]
        rot = cst[:, K_ROT:K_ROT + P]
        tri = (cst[:, K_UF:K_UF + P], cst[:, K_UB:K_UB + P])
        cosT, sinT = cst[:, K_COS:K_COS + SEG], cst[:, K_SIN:K_SIN + SEG]
        epsc = cst[:, K_EPS:K_EPS + 1]
        onec = cst[:, K_EPS + 1:K_EPS + 2]
        identb = cstb[:, 0:P]

        def mask1t(d):
            return cstb[:, B_M1T + d * P:B_M1T + (d + 1) * P]

        def mask(d, lev):
            o = B_MASK + (d * LEVELS + lev) * P
            return cstb[:, o:o + P]

        def negmask4(d):
            return cstb[:, (1 + d) * P:(2 + d) * P].rearrange("p (o n) -> p o n", o=1).to_broadcast([P, NT, P])

        def times4(ap):
            return ap.rearrange("p (o n) -> p o n", o=1).to_broadcast([P, NT, P])

        def carve(region):
            at = [0]

            def take(*shape):
                n = int(np.prod(shape))
                assert at[0] + n <= region.shape[1], (at[0], n, region.shape)
                ap = region[:, at[0]:at[0] + n]
                at[0] += n
                if len(shape) == 2:
                    ap = ap.rearrange("p (a b) -> p a b", a=shape[0])
                if len(shape) == 3:
                    ap = ap.rearrange("p (a b c) -> p a b c", a=shape[0], b=shape[1])
                if len(shape) == 4:
                    ap = ap.rearrange("p (a b c d) -> p a b c d", a=shape[0], b=shape[1], c=shape[2])
                return ap
            return take

        masks_f = arena[:, 8 * T:8 * T + NCSTB]
        spl = sb("spl", [P, NT, 48])
        take = carve(arena[:, 0:1024])
        spx, spu, spw, spt = (take(NT, 48) for _ in range(4))
        la = sb("la", [P, NT, 48])
        gcs, gtot = sb("gcs", [P, NT, 48]), sb("gtot", [P, NT, 48])
        egs, dec_end, cdk = (sb(n, [P, NT, 48]) for n in ("egs", "dec_end", "cdk"))
        dtdec = sb("dtdec", [P, NT, 32])
        beta = sb("beta", [P, NT, 16])
        gcols = sb("gcols", [P, GH, NKIND, NT * 2])
        scols = sb("scols", [P, SH, 2, NT * 2])

        take = carve(arena[:, 8 * T:32 * T])
        ED = take(2, NT, 2 * P)
        Mm, Xi, PT, decT = take(2, NT, P), take(2, NT, P), take(2, NT, P), take(2, NT, P)
        ktok, vtok, oq, osb, onb = take(NT, P), take(NT, P), take(NT, P), take(NT, P), take(NT, P)
        rbin = take(2, NT, P)
        sqb = take(2, T)
        rbuf, vnew, vdec, St = take(2, P), take(2, P), take(2, P), take(2, P)
        take = carve(work[:, :])
        qT, kT, vT, zT = take(2, T), take(2, T), take(2, T), take(2, T)
        cv = take(4, T)
        hcol, hconv, oss, ors = take(2, NKIND * NT * 2), take(2, 9), take(8), take(8)

        take = carve(work[:, :])
        xtok = take(NT, SH * SHD)
        BT, CT = take(SG, T), take(SG, T)
        xdt = take(2, NT, T)
        scv = take(2, T)
        xst = take(2, T)
        cv2 = take(2, T)
        take = carve(arena[:, 16 * T:32 * T])
        Btok = take(NT, SG, P)
        ytok = take(NT, T)
        Ex = take(2, NT, P)
        srb = take(2, NT, P)
        CBs = take(NT, P)
        Ss = take(2, T)
        stmp = take(2, T)
        sz = scv

        take = carve(work[:, :])
        akT = take(AKV, T)
        avtok = take(NT, AKV, P)
        raw = take(2, T)
        asq, arn, qn, at1 = take(T), take(T), take(T), take(SEG)
        at2 = take(SEG)
        Pm = take(2, T)
        PTm = take(NT, 2, P)
        amax, asum = take(4), take(4)
        qall = mT

        frelu = work[:, 0:8 * T].rearrange("p (a b) -> p a b", a=8)
        sgb = work[:, 0:6 * T].rearrange("p (a b) -> p a b", a=6)

        consts_in, small_in = sem("consts_in"), sem("small_in")
        masks_loaded, masks_ready = sem("masks_loaded"), sem("masks_ready")
        w_loaded = [sem(f"w_loaded{i}") for i in range(RING)]
        pieces_done = sem("pieces_done")
        small_done = sem("small_done")
        bank_free = [sem(f"bank_free{b}") for b in range(2)]
        silu_c, mod_ready = sem("silu_c"), sem("mod_ready")
        sq_ready, ss_done, rs_ready, hx_ready, h_ready = (
            sem(n) for n in ("sq_ready", "ss_done", "rs_ready", "hx_ready", "h_ready"))
        v_own, a_own, p_own = sem("v_own"), sem("a_own"), sem("p_own")
        col_v, col_a = sem("col_v"), sem("col_a")
        cv_ready, act_ready = sem("cv_ready"), sem("act_ready")
        qk_sq, qk_ss, qk_rs, qk_ready = sem("qk_sq"), sem("qk_ss"), sem("qk_rs"), sem("qk_ready")
        hcol_ready, rb_ready, m_raw, m_ready = sem("hcol_ready"), sem("rb_ready"), sem("m_raw"), sem("m_ready")
        rb_done, dec_ready, gq_done, kvt_done, kv_ready, p_ready = (
            sem(n) for n in ("rb_done", "dec_ready", "gq_done", "kvt_done", "kv_ready", "p_ready"))
        x_done, xi_ready, ed_done, ed_ready, l1_ready = (
            [sem(f"{n}{d}") for d in range(2)] for n in ("x_done", "xi_ready", "ed_done", "ed_ready", "l1_ready"))
        kq_done, r_ready, vn_done, vv_ready, sn_done, s_ready = (
            [sem(f"{n}{d}") for d in range(2)]
            for n in ("kq_done", "r_ready", "vn_done", "vv_ready", "sn_done", "s_ready"))
        o_done, o_ready, on_ready, ot_done, y_ready = (
            sem(n) for n in ("o_done", "o_ready", "on_ready", "ot_done", "y_ready"))
        t_done, t_free = sem("t_done"), sem("t_free")
        cb_done, cb_ready, xdt_ready = sem("cb_done"), sem("cb_ready"), sem("xdt_ready")
        xst_ready, st_done, sst_ready, yo_done = sem("xst_ready"), sem("st_done"), sem("sst_ready"), sem("yo_done")
        srb_ready, srb_done, ex_ready, pm_ready, diag_done = (
            sem(n) for n in ("srb_ready", "srb_done", "ex_ready", "pm_ready", "diag_done"))
        ys_sq, ys_ss, ys_rs, ys_ready = sem("ys_sq"), sem("ys_ss"), sem("ys_rs"), sem("ys_ready")
        ys_z, ysn_ready, st_free, yt_out = sem("ys_z"), sem("ysn_ready"), sem("st_free"), sem("yt_out")
        hconv_ready = sem("hconv_ready")
        n_sq, n_ss, n_rs, n_ready, r_done, rope_ready = (
            sem(n) for n in ("n_sq", "n_ss", "n_rs", "n_ready", "r_done", "rope_ready"))
        sc_done, mx_ready, e_ready, pn_ready, pt_done, pt_ready, pv_done, ya_ready = (
            sem(n) for n in ("sc_done", "mx_ready", "e_ready", "pn_ready", "pt_done", "pt_ready", "pv_done", "ya_ready"))
        m_out, a_ready = sem("m_out"), sem("a_ready")
        out_done = sem("out_done")

        block = ctx.enter_context(nc.Block())
        SCALE = float(P) ** -0.5

        @block.sync
        def _(sp):
            sp.dma_start(cst[:, :], cst_in).then_inc(consts_in, 16)
            sp.dma_start(csil[:, :, :], cvec).then_inc(consts_in, 16)
            sp.dma_start(par[:, :, :], par_in).then_inc(consts_in, 16)
            sp.dma_start(rowp[:, :, :], row_in).then_inc(consts_in, 16)
            sp.dma_start(X[:, :, :], x_in).then_inc(consts_in, 16)
            sp.dma_start(masks_f, masks_in).then_inc(masks_loaded, 16)
            sp.dma_start(wsm[:, :, :], small_w[0]).then_inc(small_in, 16)

            def load(i, k):
                sp.dma_start(ring[:, k, :, :], pieces[bass.ds(i * RING + k, 1)].rearrange(
                    "o p (a b) -> p (o a) b", a=KT)).then_inc(w_loaded[k], 16)

            for k in range(RING):
                load(0, k)
            first2 = (PIECES + N_MOD) // RING

            def passes(lo, hi):
                with sp.Fori(lo, hi) as i:
                    for k in range(RING):
                        sp.wait_ge(pieces_done, (i - 1) * RING + k + 1)
                        load(i, k)

            passes(1, first2 - 1)
            sp.wait_ge(small_done, 1)
            sp.dma_start(wsm[:, :, :], small_w[1]).then_inc(small_in, 16)
            passes(first2 - 1, DEPTH * PIECES // RING)
            for b in range(2):
                sp.wait_ge(bank_free[b], DEPTH * USES)
            sp.dma_start(out, X[:, :, SEG:T]).then_inc(out_done, 16)
            sp.wait_ge(out_done, 16)

        @block.tensor
        def _(pe):
            see = Seen(pe)
            used = [False, False]

            def dense(slot, bank, rhs, cols, first=True, last=True):
                for kk in range(KT):
                    if kk == 0:
                        pe.wait_ge(w_loaded[slot], see.next(w_loaded[slot], 16))
                        if first:
                            if used[bank]:
                                pe.wait_ge(bank_free[bank], see.next(bank_free[bank]))
                            used[bank] = True
                    mm = pe.matmul(PS[:, bank, cols], ring[:, slot, kk, :], rhs(kk)[:, cols],
                                   start=first and kk == 0, stop=last and kk == KT - 1)
                    if kk == KT - 1:
                        mm.then_inc(pieces_done, 1)
                    yield

            def run(gen):
                for _ in gen:
                    pass

            def norm_sums(cols, bank=2):
                for kk in range(KT):
                    pe.wait_ge(sq_ready, see.next(sq_ready))
                    mm = pe.matmul(PS[:, bank, cols], ones, hT[:, kk, cols], start=kk == 0, stop=kk == KT - 1)
                mm.then_inc(ss_done, 1)

            pe.wait_ge(consts_in, see.next(consts_in, 5 * 16))
            pe.wait_ge(masks_ready, 1)
            for l in range(DEPTH):
                last = l == DEPTH - 1
                every = slice(0, T)
                oc = slice(SEG, T) if last else every
                ot0 = NT // 2 if last else 0
                hk = lambda kk: hT[:, kk, :]

                if l == 0:
                    pe.wait_ge(silu_c, see.next(silu_c))
                per = {w.name: 16 for w in w_loaded}
                with see.loop(N_MOD // RING, per) as i:
                    for k in range(RING):
                        pe.wait_ge(w_loaded[k], see.next(w_loaded[k], 16))
                        for kk in range(KT):
                            mm = pe.matmul(PS[:, 7, bass.ds((i * RING + k) * 2, 2)], ring[:, k, kk, :],
                                           csil[:, kk, :], start=kk == 0, stop=kk == KT - 1)
                        mm.then_inc(pieces_done, 1)

                norm_sums(every)
                pe.wait_ge(h_ready, see.next(h_ready, KT))

                pe.wait_ge(small_in, see.next(small_in, 16))
                for t in range(NT):
                    for kk in range(KT):
                        mm = pe.matmul(PS[:, 3, t * 64:(t + 1) * 64], hT[:, kk, t * P:(t + 1) * P],
                                       wsm[:, kk, :], start=kk == 0, stop=kk == KT - 1)
                    if t < 2:
                        mm.then_inc((srb_done, diag_done)[t], 1)
                mm.then_inc(small_done, 1)
                pe.wait_ge(col_v, see.next(col_v, 3))
                laf = la[:, :, :].rearrange("p t c -> p (t c)")
                pe.matmul(PS[:, 4, 0:192], tri[0], laf, start=True, stop=True)
                pe.matmul(PS[:, 4, 192:384], tri[1], laf, start=True, stop=True)
                pe.matmul(PS[:, 5, 0:192], ones, laf, start=True, stop=True).then_inc(small_done, 1)
                pe.wait_ge(col_v, see.next(col_v, 2))

                def gdn_proj(par_):
                    for j in range(4):
                        cols = oc if j in (0, 3) else every
                        yield from dense(4 * par_ + j, j % 2, hk, cols)

                def qk_sums(par_):
                    for j in range(2):
                        pe.wait_ge(qk_sq, see.next(qk_sq))
                        if j:
                            pe.wait_ge(qk_rs, see.next(qk_rs))
                        cols = oc if j == 0 else every
                        pe.matmul(PS[:, 2, cols], ones, sqb[:, j, cols], start=True, stop=True).then_inc(qk_ss, 1)
                    pe.wait_ge(qk_rs, see.next(qk_rs))

                def gdn_head(par_, nxt):
                    fill_from = nxt if nxt is not None else iter(())

                    def fill(n):
                        for _ in range(n):
                            next(fill_from, None)

                    pe.wait_ge(act_ready, see.next(act_ready, 3))
                    pe.wait_ge(qk_ready, see.next(qk_ready, 2))
                    for t in range(NT):
                        mm = pe.transpose(PS[:, 4, t * P:(t + 1) * P], kT[:, par_, t * P:(t + 1) * P], ident)
                    mm.then_inc(kvt_done, 1)
                    for t in range(NT):
                        mm = pe.transpose(PS[:, 5, t * P:(t + 1) * P], vT[:, par_, t * P:(t + 1) * P], ident)
                    mm.then_inc(kvt_done, 1)
                    for d in range(2):
                        pe.wait_ge(rb_ready, see.next(rb_ready))
                        bank = PS[:, 2 + d, :].rearrange("p (t n) -> p t n", t=NT)
                        pe.matmul(bank, identb, negmask4(d), start=True, stop=False)
                        pe.matmul(bank, ones, rbin[:, d, :, :], start=False, stop=True).then_inc(rb_done, 1)
                    for t in range(NT):
                        tt = slice(t * P, (t + 1) * P)
                        mm = pe.matmul(PS[:, 6, tt], kT[:, par_, tt], kT[:, par_, tt], start=True, stop=True)
                    mm.then_inc(gq_done, 1)
                    for t in range(ot0, NT):
                        tt = slice(t * P, (t + 1) * P)
                        mm = pe.matmul(PS[:, 7, tt], kT[:, par_, tt], qT[:, par_, tt], start=True, stop=True)
                    mm.then_inc(gq_done, 1)
                    pe.wait_ge(m_ready, see.next(m_ready))
                    pe.wait_ge(dec_ready, see.next(dec_ready, 2))
                    for d in range(2):
                        for t in range(NT):
                            mm = pe.transpose(PS[:, 2 + d, t * P:(t + 1) * P], Mm[:, d, t, :], ident)
                        mm.then_inc(x_done[d], 1)
                    pe.wait_ge(p_ready, see.next(p_ready, 2))
                    pe.wait_ge(kv_ready, see.next(kv_ready, 2))
                    for lev in range(1, LEVELS):
                        for d in range(2):
                            if lev == 1:
                                pe.wait_ge(l1_ready[d], see.next(l1_ready[d]))
                            else:
                                pe.wait_ge(ed_ready[d], see.next(ed_ready[d]))
                            for t in range(NT):
                                mm = pe.matmul(PS[:, 2 + d, t * P:(t + 1) * P], Mm[:, d, t, :],
                                               ED[:, d, t, P:2 * P], start=True, stop=True)
                            mm.then_inc(x_done[d], 1)
                        for d in range(2):
                            pe.wait_ge(xi_ready[d], see.next(xi_ready[d]))
                            for t in range(NT):
                                if lev < LEVELS - 1:
                                    c = 2 * P * (t % 2)
                                    b = 4 + 2 * d + t // 2
                                    pe.matmul(PS[:, b, c:c + P], Xi[:, d, t, :], ED[:, d, t, 0:P],
                                              start=True, stop=True)
                                    mm = pe.matmul(PS[:, b, c + P:c + 2 * P], ED[:, d, t, 0:P], Xi[:, d, t, :],
                                                   start=True, stop=True)
                                else:
                                    mm = pe.matmul(PS[:, 4 + 2 * d, t * P:(t + 1) * P], Xi[:, d, t, :],
                                                   ED[:, d, t, 0:P], start=True, stop=True)
                            mm.then_inc(ed_done[d], 1)
                    fill(4)
                    for d in range(2):
                        pe.wait_ge(ed_ready[d], see.next(ed_ready[d]))
                    opened = False
                    for s in range(NT):
                        ts = [VISIT[d][s] for d in range(2)]
                        if s:
                            for d in range(2):
                                t = ts[d]
                                pe.wait_ge(s_ready[d], see.next(s_ready[d]))
                                mm = pe.matmul(PS[:, 4 + 2 * d, 0:P], kT[:, par_, t * P:(t + 1) * P],
                                               St[:, d, :], start=True, stop=True)
                                if t >= ot0:
                                    mm = pe.matmul(PS[:, 4 + 2 * d, P:2 * P], qT[:, par_, t * P:(t + 1) * P],
                                                   St[:, d, :], start=True, stop=True)
                                mm.then_inc(kq_done[d], 1)
                            fill(3)
                        for d in range(2):
                            t = ts[d]
                            if s:
                                pe.wait_ge(r_ready[d], see.next(r_ready[d]))
                            pe.matmul(PS[:, 5 + 2 * d, 0:P], ED[:, d, t, 0:P],
                                      rbuf[:, d, :] if s else vtok[:, t, :],
                                      start=True, stop=True).then_inc(vn_done[d], 1)
                        fill(3)
                        for d in range(2):
                            t = ts[d]
                            pe.wait_ge(vv_ready[d], see.next(vv_ready[d]))
                            if s < NT - 1:
                                pe.matmul(PS[:, 5 + 2 * d, P:2 * P], ktok[:, t, :], vdec[:, d, :],
                                          start=True, stop=True).then_inc(sn_done[d], 1)
                            if t >= ot0:
                                mm = pe.matmul(PS[:, 3, t * P:(t + 1) * P], PT[:, d, t, :], vnew[:, d, :],
                                               start=not opened, stop=s == NT - 1 and d == 1, skip_group_check=True)
                                opened = True
                        fill(2)
                    mm.then_inc(o_done, 1)
                    for _ in fill_from:
                        pass
                    if nxt is not None:
                        qk_sums(1 - par_)
                    pe.wait_ge(on_ready, see.next(on_ready))
                    for t in range(ot0, NT):
                        mm = pe.transpose(PS[:, 3, t * P:(t + 1) * P], onb[:, t, :], ident)
                    mm.then_inc(ot_done, 1)
                    pe.wait_ge(y_ready, see.next(y_ready))

                run(gdn_proj(0))
                qk_sums(0)
                per_head = {s.name: 1 for s in (m_ready, on_ready, y_ready)}
                per_head |= {s.name: 2 for s in (rb_ready, dec_ready, p_ready, kv_ready, qk_ready, qk_sq, qk_rs)}
                per_head |= {s.name: 3 for s in (act_ready,)}
                for d in range(2):
                    per_head |= {l1_ready[d].name: 1, ed_ready[d].name: LEVELS - 1, xi_ready[d].name: LEVELS - 1,
                                 s_ready[d].name: 3, r_ready[d].name: 3, vv_ready[d].name: 4, bank_free[d].name: 2}
                per = {n: 2 * v for n, v in per_head.items()} | {w.name: 16 for w in w_loaded}
                with see.loop(GH // 2 - 1, per):
                    gdn_head(0, gdn_proj(1))
                    gdn_head(1, gdn_proj(0))
                gdn_head(0, gdn_proj(1))
                gdn_head(1, None)

                def to_tokens(j):
                    pe.wait_ge(act_ready, see.next(act_ready))
                    if j >= 10:
                        return
                    if j >= 2:
                        pe.wait_ge(t_free, see.next(t_free))
                    src = scv[:, j % 2, :] if j < 8 else BT[:, j - 8, :]
                    for t in range(NT):
                        mm = pe.transpose(PS[:, 2 + j % 2, t * P:(t + 1) * P], src[:, t * P:(t + 1) * P], ident)
                    mm.then_inc(t_done, 1)

                for j in range(12):
                    run(dense(j % RING, j % 2, hk, every if j < 10 else oc))
                    if j:
                        to_tokens(j - 1)
                to_tokens(11)
                pe.wait_ge(t_free, see.next(t_free, 2))

                for g in range(SG):
                    if g:
                        pe.wait_ge(yt_out, see.next(yt_out, 4))
                    for t in range(ot0, NT):
                        tt = slice(t * P, (t + 1) * P)
                        mm = pe.matmul(PS[:, 2, tt], BT[:, g, tt], CT[:, g, tt], start=True, stop=True)
                    mm.then_inc(cb_done, 1)
                    pe.wait_ge(cb_ready, see.next(cb_ready))
                    for s in range(NT):
                        for d in range(2):
                            t = VISIT[d][s]
                            if s:
                                pe.wait_ge(sst_ready, see.next(sst_ready))
                                if t >= ot0:
                                    pe.matmul(PS[:, 4 + d, :], CT[:, g, t * P:(t + 1) * P], Ss[:, d, :],
                                              start=True, stop=True).then_inc(yo_done, 1)
                            if s < NT - 1:
                                pe.wait_ge(xst_ready, see.next(xst_ready))
                                pe.matmul(PS[:, 2 + d, :], Btok[:, t, g, :], xst[:, d, :],
                                          start=True, stop=True).then_inc(st_done, 1)
                    pe.wait_ge(st_free, see.next(st_free))
                    pe.wait_ge(xdt_ready, see.next(xdt_ready))
                    per = {srb_ready.name: 2, pm_ready.name: 1, ex_ready.name: 1}
                    with see.loop(SHG, per) as e:
                        for d in range(2):
                            pe.wait_ge(srb_ready, see.next(srb_ready))
                            bank = PS[:, 2 + d, :].rearrange("p (t n) -> p t n", t=NT)
                            pe.matmul(bank, identb, negmask4(d), start=True, stop=False)
                            mm = pe.matmul(bank, ones, srb[:, d, :, :], start=False, stop=True)
                            mm.then_inc(srb_done, 1)
                        pe.wait_ge(ex_ready, see.next(ex_ready))
                        pe.wait_ge(pm_ready, see.next(pm_ready))
                        for t in range(ot0, NT):
                            for d in range(2):
                                mm = pe.matmul(PS[:, 4 + t, bass.ds(e * SHD, SHD)], Ex[:, d, t, :],
                                               xdt[:, d, t, bass.ds(e * SHD, SHD)], start=d == 0, stop=d == 1)
                        mm.then_inc(diag_done, 1)
                    pe.wait_ge(ys_ready, see.next(ys_ready))
                    for m in range(4):
                        for t in range(ot0, NT):
                            mm = pe.transpose(PS[:, 4 + m, t * P:(t + 1) * P], ytok[:, t, m * P:(m + 1) * P], ident)
                        mm.then_inc(t_done, 1)
                pe.wait_ge(yt_out, see.next(yt_out, 4))
                for g in range(SG):
                    for m in range(4):
                        run(dense((4 + 4 * g + m) % RING, m % 2, hk, oc))
                        pe.wait_ge(ys_sq, see.next(ys_sq))
                        mm = pe.matmul(PS[:, 2 + g, oc], ones, scv[:, m % 2, oc], start=m == 0, stop=m == 3)
                        mm.then_inc(ys_ss, 1)

                for j in range(12):
                    run(dense((4 + j) % RING, j % 2, hk, every if j < 4 else oc))
                pe.wait_ge(ys_rs, see.next(ys_rs, 2))
                for j in range(AKV):
                    for t in range(NT):
                        mm = pe.transpose(PS[:, 2 + j, t * P:(t + 1) * P], raw[:, j, t * P:(t + 1) * P], ident)
                    mm.then_inc(t_done, 1)
                pe.wait_ge(t_free, see.next(t_free, AKV))

                def norm_rope(cols, dst):
                    pe.wait_ge(n_sq, see.next(n_sq))
                    pe.matmul(PS[:, 2, cols], ones, asq[:, cols], start=True, stop=True).then_inc(n_ss, 1)
                    pe.wait_ge(n_ready, see.next(n_ready))
                    pe.matmul(PS[:, 3, 0:SEG], rot, dst[:, SEG:T], start=True, stop=True).then_inc(r_done, 1)
                    pe.wait_ge(rope_ready, see.next(rope_ready))

                for j in range(AKV):
                    norm_rope(every, akT[:, j, :])
                for g in range(AKV):
                    segs = (1,) if last else (0, 1)
                    ns = len(segs)
                    per = {n_sq.name: 1, n_ready.name: 1, rope_ready.name: 1,
                           e_ready.name: 2 * ns, pn_ready.name: 2 * ns, pt_ready.name: 2 * ns, ya_ready.name: ns}
                    with see.loop(AH // AKV, per):
                        norm_rope(oc, qn)
                        for sg in segs:
                            nk = 2 * (sg + 1)
                            for q in range(2):
                                tq = (2 * sg + q) * P
                                pe.matmul(PS[:, 4 + q, 0:nk * P], qn[:, tq:tq + P], akT[:, g, 0:nk * P],
                                          start=True, stop=True).then_inc(sc_done, 1)
                            for q in range(2):
                                pe.wait_ge(e_ready, see.next(e_ready))
                                pe.wait_ge(pn_ready, see.next(pn_ready))
                                for kt in range(nk):
                                    mm = pe.transpose(PS[:, 6 + q, kt * P:(kt + 1) * P],
                                                      Pm[:, q, kt * P:(kt + 1) * P], ident)
                                mm.then_inc(pt_done, 1)
                            pe.wait_ge(pt_ready, see.next(pt_ready, 2))
                            for kt in range(nk):
                                mm = pe.matmul(PS[:, 3, 0:SEG], avtok[:, kt, g, :],
                                               PTm[:, kt, :, :].rearrange("p a b -> p (a b)"),
                                               start=kt == 0, stop=kt == nk - 1)
                            mm.then_inc(pv_done, 1)
                            pe.wait_ge(ya_ready, see.next(ya_ready))

                pe.wait_ge(ysn_ready, see.next(ysn_ready, SG))
                branch = (yG, yS, yA)
                per = {w.name: 48 for w in w_loaded} | {b.name: 12 for b in bank_free}
                with see.loop(KT // 4, per):
                    for n in range(24):
                        j = n % 6
                        y = branch[j // 2]
                        run(dense(n % RING, j % 2, (lambda kk: y[:, kk, :]) if j % 2 else hk, oc))
                pe.wait_ge(m_out, see.next(m_out, KT))
                for m in range(KT):
                    run(dense(m, m % 2, lambda kk: mT[:, kk, :], oc))
                norm_sums(oc)
                pe.wait_ge(h_ready, see.next(h_ready, KT))
                per = {w.name: 16 for w in w_loaded} | {b.name: 4 for b in bank_free}
                with see.loop(4, per):
                    for k in range(RING):
                        run(dense(k, k % 2, hk, oc))
                pe.wait_ge(a_ready, see.next(a_ready, 1 + 32))
                per = {w.name: 16 for w in w_loaded} | {b.name: 1 for b in bank_free}
                with see.loop(4, per):
                    for k in range(RING):
                        r = k % 4
                        run(dense(k, k // 4, lambda kk: aT[:, r * KT + kk, :], oc, first=r == 0, last=r == 3))

        @block.scalar
        def _(act):
            see = Seen(act)

            def ln_exp(dst, src, scale, ready, own=True):
                act.activation(dst, src, ACT.Ln, bias=epsc, scale=scale).then_inc(a_own, 1)
                act.wait_ge(a_own, see.next(a_own))
                act.activation(dst, dst, ACT.Exp, scale=-0.5).then_inc(ready, 1)

            def norm(cols, which, reads):
                if reads:
                    for b in bank_free:
                        act.wait_ge(b, see.upto(b, reads))
                for kk in range(KT):
                    act.activation(hT[:, kk, cols], X[:, kk, cols], ACT.Square).then_inc(sq_ready, 1)
                act.wait_ge(ss_done, see.next(ss_done))
                ln_exp(rs[:, cols], PS[:, 2, cols], 1.0 / D_MODEL, rs_ready)
                if which == 0:
                    act.wait_ge(mod_ready, see.next(mod_ready))
                sh = 0 if which == 0 else 24
                for kk in range(KT):
                    act.wait_ge(hx_ready, see.next(hx_ready))
                    for sg in range(2):
                        if cols.start > sg * SEG:
                            continue
                        c = slice(sg * SEG, (sg + 1) * SEG)
                        ins = act.activation(hT[:, kk, c], hT[:, kk, c], ACT.Identity,
                                             bias=modv[:, sh + kk, sg:sg + 1], scale=coefA[:, which, kk, sg:sg + 1])
                    ins.then_inc(h_ready, 1)

            act.wait_ge(consts_in, see.next(consts_in, 5 * 16))
            act.activation(csil[:, :, :], csil[:, :, :], ACT.Silu).then_inc(silu_c, 1)
            for l in range(DEPTH):
                last = l == DEPTH - 1
                every = slice(0, T)
                oc = slice(SEG, T) if last else every
                ot0 = NT // 2 if last else 0
                norm(every, 0, l * USES)
                for c in (srb_done, diag_done, a_ready):
                    see.skip(c)

                act.wait_ge(col_v, see.next(col_v))
                act.activation(spu[:, :, :], spx[:, :, :], ACT.Abs).then_inc(a_own, 1)
                act.activation(beta[:, :, :], beta[:, :, :], ACT.Exp, scale=-1.0).then_inc(col_a, 1)
                act.wait_ge(a_own, see.next(a_own))
                act.activation(spu[:, :, :], spu[:, :, :], ACT.Exp, scale=-1.0).then_inc(col_a, 1)
                act.activation(egs[:, 0, :], rowp[:, l, R_ALOG:R_ALOG + 48], ACT.Exp).then_inc(col_a, 1)
                act.wait_ge(col_v, see.next(col_v))
                act.activation(spl[:, :, :], spw[:, :, :], ACT.Ln).then_inc(col_a, 1)
                act.wait_ge(col_v, see.next(col_v, 2))
                act.activation(egs[:, :, :], gcs[:, :, :], ACT.Exp).then_inc(a_own, 1)
                act.activation(dec_end[:, :, :], dec_end[:, :, :], ACT.Exp).then_inc(a_own, 1)
                act.activation(cdk[:, :, :], gtot[:, :, :], ACT.Exp).then_inc(col_a, 1)
                see.skip(a_own, 2)
                see.skip(col_v, 1)

                def proj_evac(par_):
                    dst = (qT, kT, vT)
                    for j in range(3):
                        cols = oc if j == 0 else every
                        act.wait_ge(pieces_done, see.next(pieces_done))
                        act.activation(cv[:, j, cols], PS[:, j % 2, cols], ACT.Copy,
                                       scale=hcw(par_, 3 * j + 1)).then_inc(cv_ready, 1)
                        act.wait_ge(bank_free[j % 2], see.next(bank_free[j % 2]))
                        act.activation(dst[j][:, par_, cols], cv[:, j, cols], ACT.Silu).then_inc(act_ready, 1)
                    act.wait_ge(pieces_done, see.next(pieces_done))
                    act.activation(zT[:, par_, oc], PS[:, 1, oc], ACT.Silu).then_inc(bank_free[1], 1)
                    see.skip(bank_free[1])
                    act.wait_ge(act_ready, see.next(act_ready, 3))
                    act.activation(sqb[:, 0, oc], qT[:, par_, oc], ACT.Square).then_inc(qk_sq, 1)
                    act.activation(sqb[:, 1, :], kT[:, par_, :], ACT.Square).then_inc(qk_sq, 1)

                def qk_norm():
                    for j in range(2):
                        cols = oc if j == 0 else every
                        act.wait_ge(qk_ss, see.next(qk_ss))
                        if j:
                            act.wait_ge(qk_ready, see.next(qk_ready))
                        ln_exp(rs[:, cols], PS[:, 2, cols], 1.0, qk_rs)
                    act.wait_ge(qk_ready, see.next(qk_ready))

                def gdn_head(par_, more):
                    for j, dst in enumerate((ktok, vtok)):
                        act.wait_ge(kvt_done, see.next(kvt_done))
                        act.activation(dst, PS[:, 4 + j, :].rearrange("p (t n) -> p t n", t=NT),
                                       ACT.Copy).then_inc(kv_ready, 1)
                    act.wait_ge(hcol_ready, see.next(hcol_ready))
                    for d in range(2):
                        act.wait_ge(rb_done, see.next(rb_done))
                        for t in range(NT):
                            c = NEGG * 2 * NT + t * 2 + d
                            ins = act.activation(decT[:, d, t, :], PS[:, 2 + d, t * P:(t + 1) * P], ACT.Exp,
                                                 bias=hcol[:, par_, c:c + 1])
                        ins.then_inc(dec_ready, 1)
                    for lev in range(1, LEVELS):
                        for d in range(2):
                            act.wait_ge(ed_done[d], see.next(ed_done[d]))
                            if lev < LEVELS - 1:
                                act.activation(ED[:, d, :, :], PS[:, 4 + 2 * d:6 + 2 * d, :].rearrange(
                                    "p a (t n) -> p (a t) n", t=2), ACT.Copy).then_inc(ed_ready[d], 1)
                            else:
                                act.activation(ED[:, d, :, 0:P], PS[:, 4 + 2 * d, :].rearrange(
                                    "p (t n) -> p t n", t=NT), ACT.Copy).then_inc(ed_ready[d], 1)
                    if more:
                        proj_evac(1 - par_)
                    act.wait_ge(o_ready, see.next(o_ready))
                    for t in range(ot0, NT):
                        act.activation(onb[:, t, :], osb[:, t, :], ACT.Square,
                                       accum_out=oss[:, t:t + 1]).then_inc(a_own, 1)
                    act.wait_ge(a_own, see.next(a_own, NT - ot0))
                    act.activation(ors[:, ot0:NT], oss[:, ot0:NT], ACT.Ln, bias=epsc, scale=1.0 / P).then_inc(a_own, 1)
                    act.wait_ge(a_own, see.next(a_own))
                    act.activation(ors[:, ot0:NT], ors[:, ot0:NT], ACT.Exp, scale=-0.5).then_inc(a_own, 1)
                    act.wait_ge(a_own, see.next(a_own))
                    for t in range(ot0, NT):
                        ins = act.activation(onb[:, t, :], osb[:, t, :], ACT.Copy, scale=ors[:, t:t + 1])
                    ins.then_inc(on_ready, 1)
                    if more:
                        qk_norm()

                def hcw(par_, c):
                    return hconv[:, par_, c:c + 1]

                act.wait_ge(hconv_ready, see.next(hconv_ready))
                see.upto(pieces_done, l * PIECES + N_MOD)
                for b in bank_free:
                    see.upto(b, l * USES)
                proj_evac(0)
                qk_norm()
                nt = NT - ot0
                per_head = {pieces_done.name: 4, bank_free[0].name: 2, bank_free[1].name: 2, act_ready.name: 3, qk_ss.name: 2, qk_ready.name: 2,
                            a_own.name: 2 + nt + 2, kvt_done.name: 2, hcol_ready.name: 1, rb_done.name: 2,
                            o_ready.name: 1, hconv_ready.name: 1}
                for d in range(2):
                    per_head[ed_done[d].name] = LEVELS - 1
                with see.loop(GH // 2 - 1, {n: 2 * v for n, v in per_head.items()}):
                    for par_ in range(2):
                        act.wait_ge(hconv_ready, see.next(hconv_ready))
                        gdn_head(par_, True)
                act.wait_ge(hconv_ready, see.next(hconv_ready))
                gdn_head(0, True)
                gdn_head(1, False)

                def t_out(j):
                    if j >= 10:
                        return
                    act.wait_ge(t_done, see.next(t_done))
                    src = PS[:, 2 + j % 2, :].rearrange("p (t n) -> p t n", t=NT)
                    dst = xtok[:, :, j * P:(j + 1) * P] if j < 8 else Btok[:, :, j - 8, :]
                    act.activation(dst, src, ACT.Copy).then_inc(t_free, 1)

                act.wait_ge(y_ready, see.next(y_ready, GH))
                for j in range(12):
                    cols = every if j < 10 else oc
                    act.wait_ge(pieces_done, see.next(pieces_done))
                    act.activation(cv2[:, j % 2, cols], PS[:, j % 2, cols], ACT.Identity,
                                   bias=par[:, l, C_SCONVB + j:C_SCONVB + j + 1],
                                   scale=par[:, l, C_SCONV + 12 + j:C_SCONV + 13 + j]).then_inc(cv_ready, 1)
                    if j:
                        t_out(j - 1)
                    act.wait_ge(bank_free[j % 2], see.next(bank_free[j % 2]))
                    dst = scv[:, j % 2, :] if j < 8 else (BT[:, j - 8, :] if j < 10 else CT[:, j - 10, :])
                    act.activation(dst[:, cols], cv2[:, j % 2, cols], ACT.Silu).then_inc(act_ready, 1)
                see.skip(act_ready, 12)
                for g in range(SG):
                    act.wait_ge(cb_done, see.next(cb_done))
                    act.activation(CBs[:, ot0:NT, :], PS[:, 2, ot0 * P:T].rearrange("p (t n) -> p t n", t=NT - ot0),
                                   ACT.Copy).then_inc(cb_ready, 1)
                    with see.loop(SHG, {srb_done.name: 2, diag_done.name: 1}) as e:
                        act.wait_ge(diag_done, see.next(diag_done, 0))
                        for d in range(2):
                            act.wait_ge(srb_done, see.next(srb_done))
                            for t in range(ot0, NT):
                                c = t * 2 + d
                                ins = act.activation(
                                    Ex[:, d, t, :], PS[:, 2 + d, t * P:(t + 1) * P], ACT.Exp,
                                    bias=scols[:, bass.ds(g * SHG + e, 1), 0, c:c + 1].rearrange("p a b -> p (a b)"))
                        ins.then_inc(ex_ready, 1)
                        see.skip(diag_done)
                    for m in range(4):
                        act.wait_ge(t_done, see.next(t_done))
                        act.activation(yS[:, 4 * g + m, oc], PS[:, 4 + m, oc], ACT.Copy).then_inc(yt_out, 1)
                for g in range(SG):
                    for m in range(4):
                        act.wait_ge(pieces_done, see.next(pieces_done))
                        act.activation(scv[:, m % 2, oc], PS[:, m % 2, oc], ACT.Silu).then_inc(bank_free[m % 2], 1)
                        act.wait_ge(ys_z, see.next(ys_z))
                        act.activation(scv[:, m % 2, oc], yS[:, 4 * g + m, oc], ACT.Square).then_inc(ys_sq, 1)
                        act.wait_ge(ys_ss, see.next(ys_ss))
                    if g:
                        act.wait_ge(ysn_ready, see.next(ysn_ready))
                    ln_exp(rs[:, oc], PS[:, 2 + g, oc], 1.0 / (SHG * SHD), ys_rs)
                see.skip(ysn_ready)

                for j in range(12):
                    act.wait_ge(pieces_done, see.next(pieces_done))
                    if j < AKV:
                        dst = akT[:, j, :]
                    elif j < 2 * AKV:
                        dst = raw[:, j - AKV, :]
                    else:
                        dst = qall[:, j - 2 * AKV, oc]
                    src = PS[:, j % 2, :] if j < 2 * AKV else PS[:, j % 2, oc]
                    act.activation(dst, src, ACT.Copy).then_inc(bank_free[j % 2], 1)
                for j in range(AKV):
                    act.wait_ge(t_done, see.next(t_done))
                    act.activation(avtok[:, :, j, :], PS[:, 2 + j, :].rearrange("p (t n) -> p t n", t=NT),
                                   ACT.Copy).then_inc(t_free, 1)

                def head_norm(src, cols):
                    act.activation(asq[:, cols], src, ACT.Square).then_inc(n_sq, 1)
                    act.wait_ge(n_ss, see.next(n_ss))
                    ln_exp(arn[:, cols], PS[:, 2, cols], 1.0 / P, n_rs)

                for j in range(AKV):
                    if j:
                        act.wait_ge(n_ready, see.next(n_ready))
                    head_norm(akT[:, j, :], every)
                see.skip(n_ready, 1 + AH)
                segs = (1,) if last else (0, 1)
                ns = len(segs)
                for g in range(AKV):
                    per = {n_ss.name: 1, a_own.name: 1, mx_ready.name: 2 * ns, pt_done.name: 2 * ns,
                           pv_done.name: ns}
                    with see.loop(AH // AKV, per) as r:
                        head_norm(qall[:, bass.ds(4 * g + r, 1), oc].rearrange("p a b -> p (a b)"), oc)
                        for sg in segs:
                            nk = 2 * (sg + 1)
                            for q in range(2):
                                act.wait_ge(mx_ready, see.next(mx_ready))
                                act.activation(Pm[:, q, 0:nk * P], PS[:, 4 + q, 0:nk * P], ACT.Exp,
                                               bias=amax[:, 2 + q:3 + q], scale=SCALE,
                                               accum_out=asum[:, q:q + 1]).then_inc(e_ready, 1)
                            for q in range(2):
                                act.wait_ge(pt_done, see.next(pt_done))
                                act.activation(PTm[:, 0:nk, q, :], PS[:, 6 + q, 0:nk * P].rearrange(
                                    "p (k n) -> p k n", k=nk), ACT.Copy).then_inc(pt_ready, 1)
                            act.wait_ge(pv_done, see.next(pv_done))
                            act.activation(yA[:, bass.ds(4 * g + r, 1), sg * SEG:(sg + 1) * SEG],
                                           PS[:, 3:4, 0:SEG], ACT.Copy).then_inc(ya_ready, 1)

                with see.loop(2, {pieces_done.name: 24}):
                    for n in range(24):
                        act.wait_ge(pieces_done, see.next(pieces_done))
                        if n % 2 == 0:
                            act.activation(sgb[:, 3 * (n // 6 % 2) + n % 6 // 2, oc], PS[:, 0, oc],
                                           ACT.Sigmoid).then_inc(bank_free[0], 1)
                norm(oc, 1, l * USES + USES - U_FF1 - U_FF2)
                see.upto(pieces_done, l * PIECES + PIECES - N_FF1 - N_FF2)
                with see.loop(4, {pieces_done.name: 8, a_ready.name: 8}):
                    act.wait_ge(a_ready, see.next(a_ready, 0))
                    for k in range(RING):
                        act.wait_ge(pieces_done, see.next(pieces_done))
                        act.activation(frelu[:, k, oc], PS[:, k % 2, oc], ACT.Relu).then_inc(bank_free[k % 2], 1)
                    see.skip(a_ready, 8)

        @block.vector
        def _(dve):
            see = Seen(dve)

            def stt(out, in0, scalar, in1, op0, op1):
                return dve.scalar_tensor_tensor(out=out, in0=in0, scalar=scalar, in1=in1, op0=op0, op1=op1)

            def taps(buf, src, w0, w2, s0, bank):
                b2 = buf.rearrange("p (s n) -> p s n", s=2)
                p2 = src.rearrange("p (s n) -> p s n", s=2)
                stt(b2[:, s0:2, 1:SEG], p2[:, s0:2, 0:SEG - 1], w0, b2[:, s0:2, 1:SEG], ALU.mult, ALU.add).then_inc(v_own, 1)
                dve.wait_ge(v_own, see.next(v_own))
                stt(b2[:, s0:2, 0:SEG - 1], p2[:, s0:2, 1:SEG], w2, b2[:, s0:2, 0:SEG - 1],
                    ALU.mult, ALU.add).then_inc(bank_free[bank], 1)

            def normalise(cols):
                dve.wait_ge(rs_ready, see.next(rs_ready))
                for kk in range(KT):
                    dve.tensor_tensor(hT[:, kk, cols], X[:, kk, cols], rs[:, cols], ALU.mult).then_inc(hx_ready, 1)

            def heads_of(ap, n):
                return ap.rearrange("p (h o) -> p h o", o=1).to_broadcast([P, n, SHD])

            def by_head(ap):
                return ap.rearrange("p (h f) -> p h f", f=SHD)

            dve.wait_ge(consts_in, see.next(consts_in, 5 * 16))
            dve.wait_ge(masks_ready, 1)
            for l in range(DEPTH):
                last = l == DEPTH - 1
                every = slice(0, T)
                oc = slice(SEG, T) if last else every
                s0 = 1 if last else 0
                ot0 = NT // 2 if last else 0
                if l:
                    for b in bank_free:
                        dve.wait_ge(b, see.upto(b, l * USES))
                dve.wait_ge(pieces_done, see.upto(pieces_done, l * PIECES + N_MOD))
                bmod = par[:, l, C_BMOD:C_BMOD + 48].rearrange("p (m o) -> p m o", o=1).to_broadcast([P, 48, 2])
                dve.tensor_tensor(modv[:, :, :], PS[:, 7, 0:96].rearrange("p (m o) -> p m o", o=2), bmod, ALU.add).then_inc(v_own, 1)
                dve.wait_ge(v_own, see.next(v_own))
                for which, (c, w) in enumerate(((8, C_NMIX), (32, C_NMLP))):
                    nw = par[:, l, w:w + KT].rearrange("p (m o) -> p m o", o=1).to_broadcast([P, KT, 2])
                    ins = stt(coefA[:, which, :, :], modv[:, c:c + KT, :], 1.0, nw, ALU.add, ALU.mult)
                ins.then_inc(mod_ready, 1)
                normalise(every)

                dve.wait_ge(small_done, see.next(small_done))
                rw = PS[:, 3, 0:256].rearrange("p (t c) -> p t c", t=NT)

                def rows(o, n):
                    return rowp[:, l, o:o + n].rearrange("p (o n) -> p o n", o=1).to_broadcast([P, NT, n])

                dve.tensor_tensor(spx[:, :, :], rw[:, :, 16:64], rows(R_BIAS, 48), ALU.add)
                dve.tensor_copy(beta[:, :, :], rw[:, :, 0:16]).then_inc(col_v, 1)
                dve.wait_ge(col_a, see.next(col_a, 3))
                dve.tensor_scalar(spw[:, :, :], spu[:, :, :], 1.0, None, ALU.add).then_inc(col_v, 1)
                dve.wait_ge(col_v, see.next(col_v, 2))
                dve.tensor_scalar(spt[:, :, :], spw[:, :, :], -1.0, None, ALU.add).then_inc(v_own, 1)
                dve.wait_ge(v_own, see.next(v_own))
                dve.tensor_tensor(spt[:, :, :], spu[:, :, :], spt[:, :, :], ALU.subtract).then_inc(v_own, 1)
                dve.wait_ge(v_own, see.next(v_own))
                dve.reciprocal(gtot[:, :, :], spw[:, :, :]).then_inc(v_own, 1)
                dve.wait_ge(v_own, see.next(v_own))
                dve.tensor_tensor(spt[:, :, :], spt[:, :, :], gtot[:, :, :], ALU.mult).then_inc(v_own, 1)
                dve.wait_ge(v_own, see.next(v_own))
                dve.wait_ge(col_a, see.next(col_a))
                dve.tensor_tensor(spl[:, :, :], spl[:, :, :], spt[:, :, :], ALU.add).then_inc(v_own, 1)
                dve.wait_ge(v_own, see.next(v_own))
                stt(spl[:, :, :], spx[:, :, :], 0.0, spl[:, :, :], ALU.max, ALU.add).then_inc(v_own, 1)
                dve.wait_ge(v_own, see.next(v_own))
                ea = egs[:, 0:1, :].to_broadcast([P, NT, 48])
                stt(la[:, :, :], spl[:, :, :], -1.0, ea, ALU.mult, ALU.mult).then_inc(col_v, 1)
                dve.wait_ge(col_v, see.next(col_v))
                dve.tensor_scalar(beta[:, :, :], beta[:, :, :], 1.0, None, ALU.add).then_inc(v_own, 1)
                dve.wait_ge(v_own, see.next(v_own))
                dve.reciprocal(beta[:, :, :], beta[:, :, :]).then_inc(v_own, 1)
                dve.wait_ge(v_own, see.next(v_own))
                dve.wait_ge(small_done, see.next(small_done))
                for d in range(2):
                    cs = PS[:, 4, d * 192:(d + 1) * 192].rearrange("p (t c) -> p t c", t=NT)
                    for a, n in ((8 * d, 8), (16 + 16 * d, 16)):
                        ins = dve.tensor_copy(gcs[:, :, a:a + n], cs[:, :, a:a + n])
                ins.then_inc(a_ready, 1)
                dve.tensor_copy(gtot[:, :, :], PS[:, 5, 0:192].rearrange("p (t c) -> p t c", t=NT)).then_inc(v_own, 1)
                dve.wait_ge(v_own, see.next(v_own))
                dve.tensor_tensor(dec_end[:, :, :], gtot[:, :, :], gcs[:, :, :], ALU.subtract).then_inc(col_v, 1)
                dve.wait_ge(col_v, see.next(col_v))
                dve.wait_ge(col_a, see.next(col_a))
                for d in range(2):
                    c = slice(8 * d, 8 * d + 8)

                    def kind(k):
                        return gcols[:, :, k, :].rearrange("p h (t d) -> p d t h", d=2)[:, d]

                    dve.tensor_scalar(kind(NEGG), gcs[:, :, c], -1.0, None, ALU.mult)
                    dve.tensor_scalar(kind(NEGEG), egs[:, :, c], -1.0, None, ALU.mult)
                    dve.tensor_scalar(kind(EG), egs[:, :, c], SCALE, None, ALU.mult)
                    dve.tensor_copy(kind(BETA), beta[:, :, c])
                    dve.tensor_tensor(kind(BDEC), beta[:, :, c], dec_end[:, :, c], ALU.mult)
                    dve.tensor_copy(kind(CHUNK), cdk[:, :, c])
                    dve.tensor_copy(kind(LOGA), la[:, :, c])
                    c = slice(16 + 16 * d, 32 + 16 * d)

                    def skind(k):
                        return scols[:, :, k, :].rearrange("p h (t d) -> p d t h", d=2)[:, d]

                    dve.tensor_scalar(skind(0), gcs[:, :, c], -1.0, None, ALU.mult)
                    dve.tensor_copy(skind(1), la[:, :, c])
                dve.tensor_tensor(dtdec[:, :, :], spl[:, :, 16:48], dec_end[:, :, 16:48],
                                  ALU.mult).then_inc(col_v, 1)
                dve.wait_ge(col_v, see.next(col_v))

                def gdn_taps(par_, j):
                    if j == 0:
                        dve.wait_ge(hconv_ready, see.next(hconv_ready))
                    dve.wait_ge(cv_ready, see.next(cv_ready))
                    taps(cv[:, j, :], PS[:, j % 2, :], hconv[:, par_, 3 * j:3 * j + 1],
                         hconv[:, par_, 3 * j + 2:3 * j + 3], s0 if j == 0 else 0, j % 2)

                def qk_norm(par_):
                    for dst, cols in ((qT, oc), (kT, every)):
                        dve.wait_ge(qk_rs, see.next(qk_rs))
                        dve.tensor_tensor(dst[:, par_, cols], dst[:, par_, cols], rs[:, cols],
                                          ALU.mult).then_inc(qk_ready, 1)

                def gdn_head(h, par_, more):
                    def col(kind, t, d):
                        c = kind * 2 * NT + 2 * t + d
                        return hcol[:, par_, c:c + 1]

                    dve.wait_ge(hcol_ready, see.next(hcol_ready))
                    dve.wait_ge(gq_done, see.next(gq_done))
                    for d in range(2):
                        dve.wait_ge(dec_ready, see.next(dec_ready))
                        for t in range(NT):
                            ins = stt(Mm[:, d, t, :], PS[:, 6, t * P:(t + 1) * P], col(BETA, t, d),
                                      decT[:, d, t, :], ALU.mult, ALU.mult)
                    ins.then_inc(m_raw, 1)
                    dve.wait_ge(gq_done, see.next(gq_done))
                    for d in range(2):
                        stt(PT[:, d, ot0:NT, :], PS[:, 7, ot0 * P:T].rearrange("p (t n) -> p t n", t=NT - ot0), SCALE,
                            decT[:, d, ot0:NT, :], ALU.mult, ALU.mult).then_inc(p_ready, 1)
                    dve.wait_ge(m_ready, see.next(m_ready))
                    for d in range(2):
                        dve.tensor_tensor(ED[:, d, :, 0:P], Mm[:, d, :, :], times4(mask1t(d)), ALU.mult)
                        dve.wait_ge(x_done[d], see.next(x_done[d]))
                        dve.tensor_tensor(ED[:, d, :, P:2 * P], PS[:, 2 + d, :].rearrange(
                            "p (t n) -> p t n", t=NT), times4(mask(d, 0)), ALU.mult).then_inc(l1_ready[d], 1)
                    for lev in range(1, LEVELS):
                        for d in range(2):
                            dve.wait_ge(x_done[d], see.next(x_done[d]))
                            dve.tensor_tensor(Xi[:, d, :, :], PS[:, 2 + d, :].rearrange(
                                "p (t n) -> p t n", t=NT), times4(mask(d, lev)), ALU.mult).then_inc(xi_ready[d], 1)
                    dve.wait_ge(kv_ready, see.next(kv_ready, 2))
                    for s in range(NT):
                        ts = [VISIT[d][s] for d in range(2)]
                        if s:
                            for d in range(2):
                                dve.wait_ge(kq_done[d], see.next(kq_done[d]))
                                stt(rbuf[:, d, :], PS[:, 4 + 2 * d, 0:P], col(NEGEG, ts[d], d), vtok[:, ts[d], :],
                                    ALU.mult, ALU.add).then_inc(r_ready[d], 1)
                        for d in range(2):
                            dve.wait_ge(vn_done[d], see.next(vn_done[d]))
                            if s < NT - 1:
                                dve.tensor_scalar(vdec[:, d, :], PS[:, 5 + 2 * d, 0:P], col(BDEC, ts[d], d), None, ALU.mult)
                            dve.tensor_scalar(vnew[:, d, :], PS[:, 5 + 2 * d, 0:P], col(BETA, ts[d], d), None,
                                              ALU.mult).then_inc(vv_ready[d], 1)
                        for d in range(2):
                            t = ts[d]
                            if s and t >= ot0:
                                src = PS[:, 4 + 2 * d, P:2 * P]
                                if s < NT - 1:
                                    dve.tensor_scalar(oq[:, t, :], src, col(EG, t, d), None, ALU.mult).then_inc(v_own, 1)
                                    dve.wait_ge(v_own, see.next(v_own))
                                else:
                                    stt(oq[:, t, :], src, col(EG, t, d), oq[:, t, :], ALU.mult, ALU.add).then_inc(v_own, 1)
                                    dve.wait_ge(v_own, see.next(v_own))
                        for d in range(2):
                            if s == NT - 1:
                                continue
                            dve.wait_ge(sn_done[d], see.next(sn_done[d]))
                            new = PS[:, 5 + 2 * d, P:2 * P]
                            if s == 0:
                                dve.tensor_copy(St[:, d, :], new).then_inc(s_ready[d], 1)
                            else:
                                stt(St[:, d, :], St[:, d, :], col(CHUNK, ts[d], d), new,
                                    ALU.mult, ALU.add).then_inc(s_ready[d], 1)
                        if more and s < 3:
                            gdn_taps(1 - par_, s)
                    dve.wait_ge(o_done, see.next(o_done))
                    dve.tensor_tensor(osb[:, ot0:NT, :], PS[:, 3, ot0 * P:T].rearrange("p (t n) -> p t n", t=NT - ot0),
                                      oq[:, ot0:NT, :], ALU.add).then_inc(o_ready, 1)
                    if more:
                        qk_norm(1 - par_)
                    dve.wait_ge(ot_done, see.next(ot_done))
                    dst = yG[:, h:h + 1, oc] if isinstance(h, int) else yG[:, bass.ds(h, 1), oc]
                    stt(dst, PS[:, 3:4, oc], par[:, l, C_GNORM:C_GNORM + 1], zT[:, par_:par_ + 1, oc],
                        ALU.mult, ALU.mult).then_inc(y_ready, 1)

                for j in range(3):
                    gdn_taps(0, j)
                qk_norm(0)
                n_oq = sum(VISIT[d][s] >= ot0 for d in range(2) for s in range(1, NT))
                per_head = {hconv_ready.name: 1, cv_ready.name: 3, v_own.name: 3 + n_oq, qk_rs.name: 2,
                            hcol_ready.name: 1, dec_ready.name: 2, gq_done.name: 2, m_ready.name: 1,
                            kv_ready.name: 2, o_done.name: 1, ot_done.name: 1}
                for d in range(2):
                    per_head |= {x_done[d].name: LEVELS, kq_done[d].name: 3, vn_done[d].name: 4, sn_done[d].name: 3}
                with see.loop(GH // 2 - 1, {n: 2 * v for n, v in per_head.items()}) as i:
                    for par_ in range(2):
                        gdn_head(2 * i + par_, par_, True)
                gdn_head(GH - 2, 0, True)
                gdn_head(GH - 1, 1, False)

                for j in range(12):
                    dve.wait_ge(cv_ready, see.next(cv_ready))
                    c = C_SCONV + j
                    taps(cv2[:, j % 2, :], PS[:, j % 2, :], par[:, l, c:c + 1], par[:, l, c + 24:c + 25],
                         0 if j < 10 else s0, j % 2)
                dve.wait_ge(t_free, see.next(t_free, 10))
                for g in range(SG):
                    xg = [by_head(xtok[:, t, g * T:(g + 1) * T]) for t in range(NT)]
                    hs = [slice(16 + 16 * d + 8 * g, 24 + 16 * d + 8 * g) for d in range(2)]
                    if g:
                        dve.wait_ge(yt_out, see.next(yt_out, 4))
                    for t in range(ot0, NT):
                        ins = dve.tensor_tensor(by_head(ytok[:, t, :]), xg[t], heads_of(
                            rowp[:, l, R_SKIP + 8 * g:R_SKIP + 8 * g + 8], 8), ALU.mult)
                    ins.then_inc(v_own, 1)
                    dve.wait_ge(v_own, see.next(v_own))
                    for s in range(NT):
                        for d in range(2):
                            t = VISIT[d][s]
                            if s < NT - 1:
                                dd = slice(16 * d + 8 * g, 16 * d + 8 * g + 8)
                                dve.tensor_tensor(by_head(xst[:, d, :]), xg[t], heads_of(dtdec[:, t, dd], 8),
                                                  ALU.mult).then_inc(xst_ready, 1)
                            if s and t >= ot0:
                                dve.wait_ge(yo_done, see.next(yo_done))
                                dve.tensor_tensor(by_head(stmp[:, d, :]), by_head(PS[:, 4 + d, :]),
                                                  heads_of(egs[:, t, hs[d]], 8), ALU.mult).then_inc(v_own, 1)
                                dve.wait_ge(v_own, see.next(v_own))
                                ins = dve.tensor_tensor(ytok[:, t, :], ytok[:, t, :], stmp[:, d, :], ALU.add)
                                if (s, d) == (NT - 1, 1):
                                    ins.then_inc(st_free, 1)
                                    dve.wait_ge(st_free, see.next(st_free))
                                else:
                                    ins.then_inc(v_own, 1)
                                    dve.wait_ge(v_own, see.next(v_own))
                            if s < NT - 1:
                                dve.wait_ge(st_done, see.next(st_done))
                                if s == 0:
                                    dve.tensor_copy(Ss[:, d, :], PS[:, 2 + d, :]).then_inc(sst_ready, 1)
                                else:
                                    dve.tensor_tensor(by_head(Ss[:, d, :]), by_head(Ss[:, d, :]),
                                                      heads_of(cdk[:, t, hs[d]], 8), ALU.mult).then_inc(v_own, 1)
                                    dve.wait_ge(v_own, see.next(v_own))
                                    dve.tensor_tensor(Ss[:, d, :], Ss[:, d, :], PS[:, 2 + d, :],
                                                      ALU.add).then_inc(sst_ready, 1)
                                dve.wait_ge(sst_ready, see.next(sst_ready))
                    dve.wait_ge(cb_ready, see.next(cb_ready))
                    with see.loop(SHG, {ex_ready.name: 1}):
                        dve.wait_ge(ex_ready, see.next(ex_ready))
                        for d in range(2):
                            ins = dve.tensor_tensor(Ex[:, d, ot0:NT, :], Ex[:, d, ot0:NT, :], CBs[:, ot0:NT, :], ALU.mult)
                        ins.then_inc(pm_ready, 1)
                    dve.wait_ge(diag_done, see.next(diag_done, SHG if g else 1 + SHG))
                    for t in range(ot0, NT):
                        ins = dve.tensor_tensor(ytok[:, t, :], ytok[:, t, :], PS[:, 4 + t, :], ALU.add)
                    ins.then_inc(ys_ready, 1)
                dve.wait_ge(yt_out, see.next(yt_out, 4))
                for b in bank_free:
                    see.upto(b, l * USES + U_GDN + U_CONV)
                for g in range(SG):
                    for m in range(4):
                        dve.wait_ge(bank_free[m % 2], see.next(bank_free[m % 2]))
                        f = 4 * g + m
                        dve.tensor_tensor(yS[:, f, oc], yS[:, f, oc], scv[:, m % 2, oc], ALU.mult).then_inc(ys_z, 1)
                    dve.wait_ge(ys_rs, see.next(ys_rs))
                    for m in range(4):
                        f = 4 * g + m
                        ins = stt(yS[:, f, oc], yS[:, f, oc], par[:, l, C_SNORM + f:C_SNORM + f + 1], rs[:, oc],
                                  ALU.mult, ALU.mult)
                    ins.then_inc(ysn_ready, 1)

                def norm_rope(dst, src, cols, w):
                    dve.wait_ge(n_rs, see.next(n_rs))
                    stt(dst[:, cols], src, w, arn[:, cols], ALU.mult, ALU.mult).then_inc(n_ready, 1)
                    dve.wait_ge(n_ready, see.next(n_ready))
                    dve.tensor_tensor(at1, dst[:, SEG:T], cosT, ALU.mult)
                    dve.wait_ge(r_done, see.next(r_done))
                    dve.tensor_tensor(at2, PS[:, 3, 0:SEG], sinT, ALU.mult).then_inc(v_own, 1)
                    dve.wait_ge(v_own, see.next(v_own))
                    dve.tensor_tensor(dst[:, SEG:T], at1, at2, ALU.add).then_inc(rope_ready, 1)

                for j in range(AKV):
                    norm_rope(akT[:, j, :], akT[:, j, :], every, par[:, l, C_KN:C_KN + 1])
                segs = (1,) if last else (0, 1)
                ns = len(segs)
                for g in range(AKV):
                    per = {n_rs.name: 1, n_ready.name: 1, r_done.name: 1, v_own.name: 1 + 4 * ns,
                           sc_done.name: 2 * ns, e_ready.name: 2 * ns}
                    with see.loop(AH // AKV, per) as r:
                        norm_rope(qn, qall[:, bass.ds(4 * g + r, 1), oc].rearrange("p a b -> p (a b)"), oc,
                                  par[:, l, C_QN:C_QN + 1])
                        for sg in segs:
                            nk = 2 * (sg + 1)
                            for q in range(2):
                                dve.wait_ge(sc_done, see.next(sc_done))
                                dve.tensor_reduce(amax[:, q:q + 1], PS[:, 4 + q, 0:nk * P], AX_X, ALU.max).then_inc(v_own, 1)
                                dve.wait_ge(v_own, see.next(v_own))
                                dve.tensor_scalar(amax[:, 2 + q:3 + q], amax[:, q:q + 1], -SCALE, None,
                                                  ALU.mult).then_inc(mx_ready, 1)
                            for q in range(2):
                                dve.wait_ge(e_ready, see.next(e_ready))
                                dve.reciprocal(asum[:, 2 + q:3 + q], asum[:, q:q + 1]).then_inc(v_own, 1)
                                dve.wait_ge(v_own, see.next(v_own))
                                dve.tensor_scalar(Pm[:, q, 0:nk * P], Pm[:, q, 0:nk * P], asum[:, 2 + q:3 + q], None,
                                                  ALU.mult).then_inc(pn_ready, 1)

                for b in bank_free:
                    see.upto(b, l * USES + U_GDN + U_CONV + U_Z + U_ATT)
                see.upto(pieces_done, l * PIECES + N_MOD + N_GDN + N_SSD + N_ATT)
                with see.loop(2, {pieces_done.name: 24, bank_free[0].name: 12, bank_free[1].name: 12,
                                  v_own.name: 4}) as i:
                    for m in range(4):
                        for j in range(3):
                            b = 3 * (m % 2) + j
                            dve.wait_ge(bank_free[0], see.next(bank_free[0]))
                            dve.wait_ge(pieces_done, see.next(pieces_done, 2))
                            dve.tensor_tensor(sgb[:, b, oc], sgb[:, b, oc], PS[:, 1, oc],
                                              ALU.mult).then_inc(bank_free[1], 1)
                            dve.wait_ge(bank_free[1], see.next(bank_free[1]))
                        b = 3 * (m % 2)
                        dve.tensor_tensor(sgb[:, b, oc], sgb[:, b, oc], sgb[:, b + 1, oc], ALU.add).then_inc(v_own, 1)
                        dve.wait_ge(v_own, see.next(v_own))
                        dve.tensor_tensor(mT[:, bass.ds(4 * i + m, 1), oc], sgb[:, b:b + 1, oc],
                                          sgb[:, b + 2:b + 3, oc], ALU.add).then_inc(m_out, 1)
                for m in range(KT):
                    dve.wait_ge(pieces_done, see.next(pieces_done))
                    for sg in range(s0, 2):
                        c = slice(sg * SEG, (sg + 1) * SEG)
                        ins = stt(X[:, m, c], PS[:, m % 2, c], modv[:, 16 + m, sg:sg + 1], X[:, m, c],
                                  ALU.mult, ALU.add)
                    ins.then_inc(bank_free[m % 2], 1)
                normalise(oc)
                for b in bank_free:
                    see.upto(b, l * USES + USES - U_FF1 - U_FF2)
                with see.loop(4, {bank_free[0].name: 4, bank_free[1].name: 4}) as i:
                    for k in range(RING):
                        dve.wait_ge(bank_free[k % 2], see.next(bank_free[k % 2]))
                        dve.tensor_tensor(aT[:, bass.ds(RING * i + k, 1), oc], frelu[:, k:k + 1, oc],
                                          frelu[:, k:k + 1, oc], ALU.mult).then_inc(a_ready, 1)
                see.upto(pieces_done, l * PIECES + PIECES - N_FF2)
                with see.loop(4, {pieces_done.name: 8}) as i:
                    for m in range(2):
                        dve.wait_ge(pieces_done, see.next(pieces_done, 4))
                        for sg in range(s0, 2):
                            c = slice(sg * SEG, (sg + 1) * SEG)
                            x = X[:, bass.ds(2 * i + m, 1), c]
                            ins = stt(x, PS[:, m:m + 1, c], modv[:, bass.ds(40 + 2 * i + m, 1), sg:sg + 1].rearrange(
                                "p a b -> p (a b)"), x, ALU.mult, ALU.add)
                        ins.then_inc(bank_free[m], 1)

        @block.gpsimd
        def _(pool):
            see = Seen(pool)
            one = pool.to_reg(1.0)
            pool.wait_ge(masks_loaded, 16)
            pool.tensor_copy(cstb[:, :], masks_f).then_inc(masks_ready, 1)
            pool.wait_ge(consts_in, see.next(consts_in, 5 * 16))
            for l in range(DEPTH):
                pool.wait_ge(col_v, see.next(col_v, 5))

                def conv_weights(h, par_):
                    c = C_GCONV + 9 * h
                    src = par[:, l, c:c + 9] if isinstance(h, int) else par[:, l, bass.ds(c, 9)]
                    pool.tensor_copy(hconv[:, par_, :], src).then_inc(hconv_ready, 1)

                def gdn_head(h, par_, more):
                    src = gcols[:, h:h + 1] if isinstance(h, int) else gcols[:, bass.ds(h, 1)]
                    pool.tensor_copy(hcol[:, par_, :], src.rearrange("p o k c -> p (o k c)")).then_inc(hcol_ready, 1)
                    if more:
                        conv_weights(h + 1, 1 - par_)
                    pool.wait_ge(hcol_ready, see.next(hcol_ready))
                    for d in range(2):
                        c = LOGA * 2 * NT
                        inc = hcol[:, par_, c:c + 2 * NT].rearrange("p (t d) -> p t d", d=2)[:, :, d:d + 1]
                        pool.tensor_tensor(rbin[:, d, :, :], times4(tri[d]), inc.to_broadcast([P, NT, P]),
                                           ALU.mult).then_inc(rb_ready, 1)
                    pool.wait_ge(consts_in, 5 * 16)
                    pool.wait_ge(m_raw, see.next(m_raw))
                    mm = Mm[:, :, :, :].rearrange("p d t n -> p (d t) n")
                    pool.affine_select(out=mm, in_=mm, compare_op=ALU.not_equal, fill=one, base=0,
                                       pattern=[[0, 2 * NT], [-1, P]], channel_multiplier=1).then_inc(m_ready, 1)

                conv_weights(0, 0)
                with see.loop(GH // 2 - 1, {hcol_ready.name: 2, m_raw.name: 2}) as i:
                    for par_ in range(2):
                        gdn_head(2 * i + par_, par_, True)
                gdn_head(GH - 2, 0, True)
                gdn_head(GH - 1, 1, False)

                ot0 = NT // 2 if l == DEPTH - 1 else 0
                pool.wait_ge(t_free, see.next(t_free, 10))
                see.skip(srb_done)
                for g in range(SG):
                    for d in range(2):
                        for t in range(ot0, NT):
                            c = 16 + 16 * d + 8 * g
                            ins = pool.tensor_tensor(
                                xdt[:, d, t, :].rearrange("p (h f) -> p h f", f=SHD),
                                xtok[:, t, g * T:(g + 1) * T].rearrange("p (h f) -> p h f", f=SHD),
                                spl[:, t, c:c + 8].rearrange("p (h o) -> p h o", o=1).to_broadcast([P, 8, SHD]),
                                ALU.mult)
                    ins.then_inc(xdt_ready, 1)
                    with see.loop(SHG, {srb_done.name: 2}) as e:
                        pool.wait_ge(srb_done, see.next(srb_done, 0))
                        for d in range(2):
                            inc = scols[:, bass.ds(g * SHG + e, 1), 1, :].rearrange(
                                "p o (t d) -> p (o t) d", d=2)[:, :, d:d + 1]
                            pool.tensor_tensor(srb[:, d, :, :], times4(tri[d]), inc.to_broadcast([P, NT, P]),
                                               ALU.mult).then_inc(srb_ready, 1)
                        see.skip(srb_done, 2)
                    pool.wait_ge(diag_done, see.next(diag_done, SHG if g else 1 + SHG))
                pool.wait_ge(t_free, see.next(t_free, AKV))



def _constants():
    c = np.zeros((P, NCST), np.float32)
    i = np.arange(P)
    c[:, K_ID:K_ID + P] = np.eye(P)
    c[:, K_ONES:K_ONES + P] = 1
    c[:, K_UF:K_UF + P] = i[:, None] <= i[None, :]
    c[:, K_UB:K_UB + P] = i[:, None] >= i[None, :]
    for o in (0, 64):
        for j in range(32):
            c[o + 32 + j, K_ROT + o + j] = -1
            c[o + j, K_ROT + o + 32 + j] = 1
    tok = np.arange(SEG)
    freq = np.float32(10000.0) ** (-np.arange(32, dtype=np.float32) / np.float32(32))
    for o, pos in ((0, tok // GRID_W), (64, tok % GRID_W)):
        ang = (pos.astype(np.float32)[None, :] * freq[:, None]).astype(np.float32)
        for k in (0, 32):
            c[o + k:o + k + 32, K_COS:K_COS + SEG] = np.cos(ang)
            c[o + k:o + k + 32, K_SIN:K_SIN + SEG] = np.sin(ang)
    c[:, K_EPS] = EPS
    c[:, K_EPS + 1] = 1
    b16 = np.zeros((P, NCSTB), np.float32)
    for lev in range(LEVELS):
        b = 1 << lev
        low = (i[:, None] // (2 * b) == i[None, :] // (2 * b)) & (i[:, None] % (2 * b) >= b) & (i[None, :] % (2 * b) < b)
        m = np.eye(P) - low
        for d, md in enumerate((m, m.T)):
            o = B_MASK + (d * LEVELS + lev) * P
            b16[:, o:o + P] = md
            if lev == 0:
                b16[:, B_M1T + d * P:B_M1T + (d + 1) * P] = md.T
    b16[:, 0:P] = np.eye(P)
    b16[:, P:2 * P] = np.where(i[:, None] <= i[None, :], 0, -1e30)
    b16[:, 2 * P:3 * P] = np.where(i[:, None] >= i[None, :], 0, -1e30)
    return c, b16


def _cut(w):
    r, m = w.shape[0] // D_MODEL, w.shape[1] // P
    return w.reshape(r, KT, P, m, P).transpose(0, 3, 2, 1, 4).reshape(r, m, P, KT * P)


def _pieces(w_mod, w_in, w_br, w_out, w_ff1, w_ff2):
    def cols(o, n=P):
        return w_in[:, o:o + n]

    out = [_cut(w_mod)[0]]
    o_z, o_sz, o_xbc, o_q, o_kv, o_gate = 3072, 4128, 5152, 6720, 7744, 8256
    for h in range(GH):
        out += [_cut(cols(o))[0] for o in (h * P, 1024 + h * P, 2048 + h * P, o_z + h * P)]
    out += [_cut(cols(o_xbc, 1536))[0], _cut(cols(o_sz, 1024))[0]]
    out += [_cut(cols(o_kv, 512))[0], _cut(cols(o_q, 1024))[0]]
    for m in range(KT):
        for b in range(3):
            out += [_cut(cols(o_gate + b * D_MODEL + m * P))[0], _cut(w_br[b][:, m * P:(m + 1) * P])[0]]
    out += [_cut(w_out)[0], _cut(w_ff1)[0]]
    out += [_cut(w_ff2).transpose(1, 0, 2, 3).reshape(-1, P, KT * P)]
    return np.concatenate(out, 0)


def kernel(x, c, ctx, c_ctx, w_mod, b_mod, norm_mix, norm_mlp, w_in, gdn_conv, gdn_a_log, gdn_dt_bias,
           gdn_norm, ssd_conv_w, ssd_conv_b, ssd_a_log, ssd_dt_bias, ssd_d, ssd_norm, att_q_norm, att_k_norm,
           w_br_gdn, w_br_ssd, w_br_att, w_out, w_ff1, w_ff2):
    import concourse.bacc as bacc
    from concourse.bass_utils import run_bass_kernel_spmd

    a = {n: np.asarray(v) for n, v in dict(
        x=x, c=c, ctx=ctx, c_ctx=c_ctx, w_mod=w_mod, b_mod=b_mod, norm_mix=norm_mix, norm_mlp=norm_mlp, w_in=w_in,
        gdn_conv=gdn_conv, gdn_a_log=gdn_a_log, gdn_dt_bias=gdn_dt_bias, gdn_norm=gdn_norm, ssd_conv_w=ssd_conv_w,
        ssd_conv_b=ssd_conv_b, ssd_a_log=ssd_a_log, ssd_dt_bias=ssd_dt_bias, ssd_d=ssd_d, ssd_norm=ssd_norm,
        att_q_norm=att_q_norm, att_k_norm=att_k_norm, w_br_gdn=w_br_gdn, w_br_ssd=w_br_ssd, w_br_att=w_br_att,
        w_out=w_out, w_ff1=w_ff1, w_ff2=w_ff2).items()}
    L = range(DEPTH)
    pieces = np.concatenate([_pieces(a["w_mod"][l], a["w_in"][l], (a["w_br_gdn"][l], a["w_br_ssd"][l],
                                                                   a["w_br_att"][l]),
                                     a["w_out"][l], a["w_ff1"][l], a["w_ff2"][l]) for l in L])
    o_beta, o_dt = 4096, 6688
    small = np.stack([np.concatenate([a["w_in"][l][:, o_beta:o_beta + 32], a["w_in"][l][:, o_dt:o_dt + 32]], 1)
                      .reshape(KT, P, 64).transpose(1, 0, 2) for l in L])
    tokens = np.concatenate([a["ctx"][0], a["x"][0]], 0)
    x_in = np.ascontiguousarray(tokens.reshape(T, KT, P).transpose(2, 1, 0))
    cvec = np.ascontiguousarray(np.stack([a["c_ctx"], a["c"][0]]).reshape(2, KT, P).transpose(2, 1, 0))
    par_in = []
    for l in L:
        gconv = a["gdn_conv"][l].reshape(3, 3, GH, P).transpose(2, 1, 0, 3).reshape(72, P)
        par_in.append(np.concatenate([
            a["b_mod"][l].reshape(-1, P), a["norm_mix"][l].reshape(-1, P), a["norm_mlp"][l].reshape(-1, P), gconv,
            a["ssd_conv_w"][l].reshape(36, P), a["ssd_conv_b"][l].reshape(12, P), a["ssd_norm"][l].reshape(8, P),
            a["gdn_norm"][l][None], a["att_q_norm"][l][None], a["att_k_norm"][l][None]]).T)
    par_in = np.ascontiguousarray(np.stack(par_in, 1))
    row = np.stack([np.concatenate([a[n][l].reshape(-1) for n in (
        "gdn_dt_bias", "ssd_dt_bias", "gdn_a_log", "ssd_a_log", "ssd_d")]) for l in L])
    row_in = np.ascontiguousarray(np.broadcast_to(row[None], (P, DEPTH, NROW)))
    cst, masks = _constants()

    nc = bacc.Bacc("TRN2", target_bir_lowering=False, num_devices=1)
    arrays = {"pieces": pieces, "small_w": np.ascontiguousarray(small), "x_in": x_in, "cvec": cvec,
              "par_in": par_in, "row_in": row_in, "cst_in": cst, "masks_in": masks}
    aps = [nc.dram_tensor(n, v.shape, mybir.dt.from_np(v.dtype), kind="ExternalInput").ap() for n, v in arrays.items()]
    aps.append(nc.dram_tensor("out", (P, KT, SEG), F32, kind="ExternalOutput").ap())
    build(nc, *aps)
    got = run_bass_kernel_spmd(nc, [arrays], core_ids=[0]).results[0]["out"]
    return np.ascontiguousarray(np.asarray(got).transpose(2, 1, 0).reshape(1, SEG, D_MODEL))
```
